# Optimizing a Trainium2 kernel written in Bass

```python
import math
import jax, jax.numpy as jnp
from jax import lax
import numpy as np

D_MODEL = 1024
BATCH = 1
SEQ = 256
DEPTH = 2

HEAD_DIM = 64
HEADS_PER_GROUP = 4
GROUP_WIDTH = HEADS_PER_GROUP * HEAD_DIM
N_MIXERS = 4
D_MIX = N_MIXERS * GROUP_WIDTH

MLA_Q_RANK = 192
MLA_KV_RANK = 128
MLA_NOPE_DIM = HEAD_DIM
MLA_ROPE_DIM = 32
MLA_V_DIM = HEAD_DIM
ROPE_THETA = 10000.0

Q_BLOCK = 128

MOBA_BLOCK = 256
MOBA_TOPK = 3
MOBA_Q_CHUNK = 32

CONV_WIDTH = 31

NUM_BUCKETS = 32
MAX_DISTANCE = 1024

NORM_EPS = 1e-6

COLS_MLA = MLA_Q_RANK + MLA_KV_RANK + MLA_ROPE_DIM
COLS_SB = 3 * GROUP_WIDTH
COLS_MOBA = 3 * GROUP_WIDTH
COLS_CONV = 2 * GROUP_WIDTH
COLS_GATE = D_MIX
D_IN_PROJ = COLS_MLA + COLS_SB + COLS_MOBA + COLS_CONV + COLS_GATE
SPLITS = [COLS_MLA, COLS_MLA + COLS_SB, COLS_MLA + COLS_SB + COLS_MOBA,
          COLS_MLA + COLS_SB + COLS_MOBA + COLS_CONV]


def rms_norm(x, g):
    x32 = x.astype(jnp.float32)
    y = x32 * lax.rsqrt(jnp.mean(x32 * x32, axis=-1, keepdims=True) + NORM_EPS)
    return (y * g.astype(jnp.float32)).astype(x.dtype)

def layer_norm(x, g, b):
    x32 = x.astype(jnp.float32)
    mu = jnp.mean(x32, axis=-1, keepdims=True)
    xc = x32 - mu
    var = jnp.mean(xc * xc, axis=-1, keepdims=True)
    y = xc * lax.rsqrt(var + NORM_EPS)
    return (y * g.astype(jnp.float32) + b.astype(jnp.float32)).astype(x.dtype)

def split_heads(t, n_heads):
    B, S, E = t.shape
    return t.reshape(B, S, n_heads, E // n_heads).transpose(0, 2, 1, 3)

def merge_heads(t):
    B, H, S, d = t.shape
    return t.transpose(0, 2, 1, 3).reshape(B, S, H * d)

def to_blocks(t, blk):
    B, H, S, d = t.shape
    return t.reshape(B, H, S // blk, blk, d).transpose(2, 0, 1, 3, 4)

def from_blocks(t):
    n, B, H, blk, d = t.shape
    return t.transpose(1, 2, 0, 3, 4).reshape(B, H, n * blk, d)

def rope_tables(pos):
    half = MLA_ROPE_DIM // 2
    freqs = ROPE_THETA ** (-jnp.arange(half, dtype=jnp.float32) / half)
    ang = pos.astype(jnp.float32)[:, None] * freqs[None, :]
    return jnp.cos(ang), jnp.sin(ang)

def apply_rope(x, cos, sin):
    half = x.shape[-1] // 2
    c = cos.astype(x.dtype)
    s = sin.astype(x.dtype)
    x1, x2 = x[..., :half], x[..., half:]
    return jnp.concatenate([x1 * c - x2 * s, x1 * s + x2 * c], axis=-1)

def t5_bucket(dist):
    n = jnp.maximum(dist, 0)
    max_exact = NUM_BUCKETS // 2
    n_large = jnp.maximum(n, max_exact).astype(jnp.float32)
    large = max_exact + (jnp.log(n_large / max_exact) / math.log(MAX_DISTANCE / max_exact)
                         * (NUM_BUCKETS - max_exact)).astype(jnp.int32)
    large = jnp.minimum(large, NUM_BUCKETS - 1)
    return jnp.where(n < max_exact, n, large)

def mla_attention(q_nope, q_rope, k_nope, k_rope, v):
    S = q_nope.shape[2]
    scale = (MLA_NOPE_DIM + MLA_ROPE_DIM) ** -0.5
    key_pos = jnp.arange(S, dtype=jnp.int32)

    def one_block(args):
        qn_b, qr_b, i = args
        s = (jnp.einsum('bhqd,bhkd->bhqk', qn_b, k_nope)
             + jnp.einsum('bhqd,bkd->bhqk', qr_b, k_rope)).astype(jnp.float32) * scale
        qpos = i * Q_BLOCK + jnp.arange(Q_BLOCK, dtype=jnp.int32)
        s = jnp.where(key_pos[None, :] <= qpos[:, None], s, -jnp.inf)
        p = jax.nn.softmax(s, axis=-1).astype(v.dtype)
        return jnp.einsum('bhqk,bhkd->bhqd', p, v)

    n = S // Q_BLOCK
    out = lax.map(one_block, (to_blocks(q_nope, Q_BLOCK), to_blocks(q_rope, Q_BLOCK),
                              jnp.arange(n, dtype=jnp.int32)))
    return from_blocks(out)

def stick_breaking_attention(q, k, v):
    S = q.shape[2]
    scale = q.shape[-1] ** -0.5
    key_pos = jnp.arange(S, dtype=jnp.int32)

    def one_block(args):
        q_b, i = args
        z = jnp.einsum('bhqd,bhkd->bhqk', q_b, k).astype(jnp.float32) * scale
        qpos = i * Q_BLOCK + jnp.arange(Q_BLOCK, dtype=jnp.int32)
        past = key_pos[None, :] < qpos[:, None]
        log_beta = jax.nn.log_sigmoid(z)
        log_1m_beta = jnp.where(past, jax.nn.log_sigmoid(-z), 0.0)
        suffix = lax.cumsum(log_1m_beta, axis=3, reverse=True) - log_1m_beta
        a = jnp.where(past, jnp.exp(log_beta + suffix), 0.0).astype(v.dtype)
        return jnp.einsum('bhqk,bhkd->bhqd', a, v)

    n = S // Q_BLOCK
    out = lax.map(one_block, (to_blocks(q, Q_BLOCK), jnp.arange(n, dtype=jnp.int32)))
    return from_blocks(out)

def moba_attention(q, k, v, rel_bias):
    B, H, S, d = q.shape
    nb = -(-S // MOBA_BLOCK)
    pad = nb * MOBA_BLOCK - S
    k_p = jnp.pad(k, ((0, 0), (0, 0), (0, pad), (0, 0)))
    v_p = jnp.pad(v, ((0, 0), (0, 0), (0, pad), (0, 0)))
    k_blocks = k_p.reshape(B, H, nb, MOBA_BLOCK, d)
    v_blocks = v_p.reshape(B, H, nb, MOBA_BLOCK, d)
    k_mean = jnp.mean(k_blocks.astype(jnp.float32), axis=3)
    top_k = min(MOBA_TOPK, nb)
    scale = d ** -0.5
    offs = jnp.arange(MOBA_BLOCK, dtype=jnp.int32)
    blk_ids = jnp.arange(nb, dtype=jnp.int32)
    bi = jnp.arange(B)[:, None, None, None]
    hi = jnp.arange(H)[None, :, None, None]
    bias_t = rel_bias.T

    def one_chunk(args):
        q_c, i = args
        start = i * MOBA_Q_CHUNK
        qpos = start + jnp.arange(MOBA_Q_CHUNK, dtype=jnp.int32)
        own_blk = start // MOBA_BLOCK
        gate = jnp.einsum('bhqd,bhnd->bhqn', q_c.astype(jnp.float32), k_mean)
        gate = jnp.where((blk_ids < own_blk)[None, :], gate, -jnp.inf)
        _, idx = lax.top_k(gate, top_k)
        valid = idx < own_blk
        k_sel = k_blocks[bi, hi, idx]
        v_sel = v_blocks[bi, hi, idx]
        s_sel = jnp.einsum('bhqd,bhqkcd->bhqkc', q_c, k_sel).astype(jnp.float32) * scale
        kpos_sel = idx[..., None] * MOBA_BLOCK + offs
        s_sel = s_sel + bias_t[hi[..., None], t5_bucket(qpos[:, None, None] - kpos_sel)]
        s_sel = jnp.where(valid[..., None], s_sel, -jnp.inf)
        s_sel = s_sel.reshape(B, H, MOBA_Q_CHUNK, top_k * MOBA_BLOCK)
        k_own = lax.dynamic_slice_in_dim(k_p, own_blk * MOBA_BLOCK, MOBA_BLOCK, axis=2)
        v_own = lax.dynamic_slice_in_dim(v_p, own_blk * MOBA_BLOCK, MOBA_BLOCK, axis=2)
        dist_own = qpos[:, None] - (own_blk * MOBA_BLOCK + offs)[None, :]
        s_own = (jnp.einsum('bhqd,bhcd->bhqc', q_c, k_own).astype(jnp.float32) * scale
                 + bias_t[:, t5_bucket(dist_own)])
        s_own = jnp.where(dist_own >= 0, s_own, -jnp.inf)
        p = jax.nn.softmax(jnp.concatenate([s_sel, s_own], axis=-1), axis=-1).astype(v.dtype)
        p_sel = p[..., :top_k * MOBA_BLOCK].reshape(B, H, MOBA_Q_CHUNK, top_k, MOBA_BLOCK)
        p_own = p[..., top_k * MOBA_BLOCK:]
        return (jnp.einsum('bhqkc,bhqkcd->bhqd', p_sel, v_sel)
                + jnp.einsum('bhqc,bhcd->bhqd', p_own, v_own))

    n = S // MOBA_Q_CHUNK
    out = lax.map(one_chunk, (to_blocks(q, MOBA_Q_CHUNK), jnp.arange(n, dtype=jnp.int32)))
    return from_blocks(out)

def conformer_conv(u, dw_w, dw_b, ln_g, ln_b, pw_w, pw_b):
    a, g = jnp.split(u, 2, axis=-1)
    xg = a * jax.nn.sigmoid(g)
    y = lax.conv_general_dilated(
        xg, dw_w[:, None, :].astype(xg.dtype), window_strides=(1,),
        padding=[(CONV_WIDTH - 1, 0)], dimension_numbers=('NWC', 'WIO', 'NWC'),
        feature_group_count=GROUP_WIDTH) + dw_b
    y = jax.nn.silu(layer_norm(y, ln_g, ln_b))
    return jnp.einsum('bsc,ce->bse', y, pw_w) + pw_b

def first_inputs(seed: int = 0) -> dict:
    key = jax.random.key(seed)
    ks = jax.random.split(key, 16)
    f32 = jnp.float32

    def nrm(k, shape, fan_in):
        return jax.random.normal(k, shape, f32) * (fan_in ** -0.5)

    def gain(k, shape):
        return 1.0 + 0.05 * jax.random.normal(k, shape, f32)

    return {
        "x": jax.random.normal(ks[0], (BATCH, SEQ, D_MODEL), f32),
        "pre_norm_g": gain(ks[1], (DEPTH, D_MODEL)),
        "w_in": nrm(ks[2], (DEPTH, D_MODEL, D_IN_PROJ), D_MODEL),
        "mla_q_norm_g": gain(ks[3], (DEPTH, MLA_Q_RANK)),
        "mla_w_uq": nrm(ks[4], (DEPTH, MLA_Q_RANK, HEADS_PER_GROUP * (MLA_NOPE_DIM + MLA_ROPE_DIM)), MLA_Q_RANK),
        "mla_kv_norm_g": gain(ks[5], (DEPTH, MLA_KV_RANK)),
        "mla_w_ukv": nrm(ks[6], (DEPTH, MLA_KV_RANK, HEADS_PER_GROUP * (MLA_NOPE_DIM + MLA_V_DIM)), MLA_KV_RANK),
        "rel_bias": 0.2 * jax.random.normal(ks[7], (NUM_BUCKETS, HEADS_PER_GROUP), f32),
        "conv_dw_w": nrm(ks[8], (DEPTH, CONV_WIDTH, GROUP_WIDTH), CONV_WIDTH),
        "conv_dw_b": 0.02 * jax.random.normal(ks[9], (DEPTH, GROUP_WIDTH), f32),
        "conv_ln_g": gain(ks[10], (DEPTH, GROUP_WIDTH)),
        "conv_ln_b": 0.02 * jax.random.normal(ks[11], (DEPTH, GROUP_WIDTH), f32),
        "conv_pw_w": nrm(ks[12], (DEPTH, GROUP_WIDTH, GROUP_WIDTH), GROUP_WIDTH),
        "conv_pw_b": 0.02 * jax.random.normal(ks[13], (DEPTH, GROUP_WIDTH), f32),
        "w_out": nrm(ks[14], (DEPTH, D_MIX, D_MODEL), D_MIX),
        "post_norm_g": gain(ks[15], (DEPTH, D_MODEL)),
    }

def first_block(x, pre_norm_g, w_in, mla_q_norm_g, mla_w_uq, mla_kv_norm_g, mla_w_ukv,
              rel_bias, conv_dw_w, conv_dw_b, conv_ln_g, conv_ln_b, conv_pw_w, conv_pw_b,
              w_out, post_norm_g):
    S = x.shape[1]
    cos, sin = rope_tables(jnp.arange(S, dtype=jnp.int32))
    H = HEADS_PER_GROUP
    for l in range(DEPTH):
        h = rms_norm(x, pre_norm_g[l])
        u = jnp.einsum('bsd,de->bse', h, w_in[l])
        u_mla, u_sb, u_moba, u_conv, u_gate = jnp.split(u, SPLITS, axis=-1)

        c_q, c_kv, k_rope_raw = jnp.split(u_mla, [MLA_Q_RANK, MLA_Q_RANK + MLA_KV_RANK], axis=-1)
        qa = split_heads(jnp.einsum('bsr,re->bse', rms_norm(c_q, mla_q_norm_g[l]), mla_w_uq[l]), H)
        q_nope = qa[..., :MLA_NOPE_DIM]
        q_rope = apply_rope(qa[..., MLA_NOPE_DIM:], cos, sin)
        kva = split_heads(jnp.einsum('bsr,re->bse', rms_norm(c_kv, mla_kv_norm_g[l]), mla_w_ukv[l]), H)
        k_nope = kva[..., :MLA_NOPE_DIM]
        v_a = kva[..., MLA_NOPE_DIM:]
        k_rope = apply_rope(k_rope_raw, cos, sin)
        o_a = merge_heads(mla_attention(q_nope, q_rope, k_nope, k_rope, v_a))

        qb, kb, vb = jnp.split(u_sb, 3, axis=-1)
        o_b = merge_heads(stick_breaking_attention(split_heads(qb, H), split_heads(kb, H), split_heads(vb, H)))

        qc, kc, vc = jnp.split(u_moba, 3, axis=-1)
        o_c = merge_heads(moba_attention(split_heads(qc, H), split_heads(kc, H), split_heads(vc, H), rel_bias))

        o_d = conformer_conv(u_conv, conv_dw_w[l], conv_dw_b[l], conv_ln_g[l], conv_ln_b[l],
                             conv_pw_w[l], conv_pw_b[l])

        y = jnp.concatenate([o_a, o_b, o_c, o_d], axis=-1) * jax.nn.silu(u_gate)
        y = jnp.einsum('bse,ed->bsd', y, w_out[l])
        x = x + rms_norm(y, post_norm_g[l])
    return x


CHUNK = 64
N_MIXERS_2 = 2
GLA_HEADS = 4
GLA_DK = D_MODEL // 2
GLA_DV = D_MODEL
GLA_DK_HEAD = GLA_DK // GLA_HEADS
GLA_DV_HEAD = GLA_DV // GLA_HEADS
GLA_GATE_RANK = 16
GLA_GATE_TAU = 16.0
GLA_IN_WIDTH = 2 * GLA_DK + 2 * GLA_DV + GLA_GATE_RANK
ATT_HEADS = 16
ATT_HEAD_DIM = D_MODEL // ATT_HEADS
LEFT_CHUNKS = 8
BAND = (LEFT_CHUNKS + 1) * CHUNK
MAX_REL = 128
N_REL = 2 * MAX_REL + 1
D_FF = 4 * D_MODEL
DEEPNORM_ALPHA = (2.0 * DEPTH) ** 0.25
DEEPNORM_BETA = (8.0 * DEPTH) ** -0.25
LN_EPS = 1e-5
RMS_EPS = 1e-6
NEG_INF = -1e30
N_GLA_LAYERS = (DEPTH + 1) // 2
N_ATT_LAYERS = DEPTH // 2


def layer_norm_2(x, g, b):
    xf = x.astype(jnp.float32)
    mu = jnp.mean(xf, -1, keepdims=True)
    var = jnp.mean(jnp.square(xf - mu), -1, keepdims=True)
    return ((xf - mu) * lax.rsqrt(var + LN_EPS)).astype(x.dtype) * g + b

def gla_mixer(u, w_in, w_gk2, b_gk, g_norm, w_out):
    B_, S_, _ = u.shape
    nC = S_ // CHUNK
    proj = u @ w_in
    q, k, v, g, gk_lr = jnp.split(
        proj, [GLA_DK, 2 * GLA_DK, 2 * GLA_DK + GLA_DV, 2 * GLA_DK + 2 * GLA_DV], axis=-1)
    log_a = jax.nn.log_sigmoid((gk_lr @ w_gk2 + b_gk).astype(jnp.float32)) / GLA_GATE_TAU

    def to_chunks(t, hd):
        return t.reshape(B_, nC, CHUNK, GLA_HEADS, hd).transpose(0, 3, 1, 2, 4)

    qc = to_chunks(q.astype(jnp.float32), GLA_DK_HEAD) * (GLA_DK_HEAD ** -0.5)
    kc = to_chunks(k.astype(jnp.float32), GLA_DK_HEAD)
    vc = to_chunks(v.astype(jnp.float32), GLA_DV_HEAD)
    cum = jnp.cumsum(to_chunks(log_a, GLA_DK_HEAD), axis=3)
    e_pos = jnp.exp(cum)
    e_neg = jnp.exp(-cum)
    q_fwd = qc * e_pos
    a_fwd = jnp.einsum('bhntd,bhnsd->bhnts', q_fwd, kc * e_neg)
    a_bwd = jnp.einsum('bhntd,bhnsd->bhnts', qc * e_neg, kc * e_pos)
    lower = jnp.tril(jnp.ones((CHUNK, CHUNK), dtype=bool))
    o_intra = jnp.einsum('bhnts,bhnsv->bhntv', jnp.where(lower, a_fwd, a_bwd), vc)
    k_to_end = kc * jnp.exp(cum[:, :, :, -1:, :] - cum)
    chunk_decay = jnp.exp(cum[:, :, :, -1, :])

    def step(state, inp):
        qs, ke, vv, dec = inp
        o = jnp.einsum('bhtk,bhkv->bhtv', qs, state)
        state = state * dec[..., None] + jnp.einsum('bhtk,bhtv->bhkv', ke, vv)
        return state, o

    s0 = jnp.zeros((B_, GLA_HEADS, GLA_DK_HEAD, GLA_DV_HEAD), jnp.float32)
    _, o_inter = lax.scan(step, s0, (jnp.moveaxis(q_fwd, 2, 0), jnp.moveaxis(k_to_end, 2, 0),
                                     jnp.moveaxis(vc, 2, 0), jnp.moveaxis(chunk_decay, 2, 0)))
    o = o_intra + jnp.moveaxis(o_inter, 0, 2)
    o = o * lax.rsqrt(jnp.mean(jnp.square(o), -1, keepdims=True) + RMS_EPS)
    o = o * g_norm.astype(jnp.float32)[None, :, None, None, :]
    o = o.transpose(0, 2, 3, 1, 4).reshape(B_, S_, GLA_DV).astype(u.dtype)
    return (o * jax.nn.silu(g)) @ w_out

def chunk_attention(u, w_in, b_in, rel_bias, w_out):
    B_, S_, _ = u.shape
    nC = S_ // CHUNK
    q, k, v = jnp.split(u @ w_in + b_in, 3, axis=-1)

    def heads(t):
        return t.reshape(B_, S_, ATT_HEADS, ATT_HEAD_DIM).transpose(0, 2, 1, 3)

    pad = LEFT_CHUNKS * CHUNK
    qc = (heads(q) * (ATT_HEAD_DIM ** -0.5)).reshape(B_, ATT_HEADS, nC, CHUNK, ATT_HEAD_DIM)
    kp = jnp.pad(heads(k), ((0, 0), (0, 0), (pad, 0), (0, 0)))
    vp = jnp.pad(heads(v), ((0, 0), (0, 0), (pad, 0), (0, 0)))
    key_valid = jnp.arange(S_ + pad) >= pad
    rel = jnp.clip(pad + jnp.arange(CHUNK)[:, None] - jnp.arange(BAND)[None, :], -MAX_REL, MAX_REL) + MAX_REL
    bias = rel_bias.astype(jnp.float32)[:, rel]

    def one_chunk(inp):
        qi, start = inp
        kb = lax.dynamic_slice_in_dim(kp, start, BAND, axis=2)
        vb = lax.dynamic_slice_in_dim(vp, start, BAND, axis=2)
        mb = lax.dynamic_slice_in_dim(key_valid, start, BAND)
        s = jnp.einsum('bhtd,bhjd->bhtj', qi, kb).astype(jnp.float32) + bias
        p = jax.nn.softmax(jnp.where(mb, s, NEG_INF), axis=-1).astype(vb.dtype)
        return jnp.einsum('bhtj,bhjd->bhtd', p, vb)

    o = lax.map(one_chunk, (jnp.moveaxis(qc, 2, 0), jnp.arange(nC) * CHUNK))
    o = o.transpose(1, 0, 3, 2, 4).reshape(B_, S_, D_MODEL)
    return o @ w_out

def squared_relu_mlp(u, w1, w2):
    return jnp.square(jax.nn.relu(u @ w1)) @ w2

def second_inputs(seed: int = 0) -> dict:
    key = jax.random.key(seed)
    ks = jax.random.split(key, 16)
    nrm = lambda k, shape, s: jax.random.normal(k, shape, jnp.float32) * s
    D = D_MODEL
    return {
        "x": nrm(ks[0], (BATCH, SEQ, D), 1.0),
        "c": nrm(ks[1], (BATCH, D), 1.0),
        "w_ada": nrm(ks[2], (DEPTH, D, 6 * D), 0.1 * D ** -0.5),
        "b_ada": nrm(ks[3], (DEPTH, 6 * D), 0.02),
        "ln_g": 1.0 + nrm(ks[4], (DEPTH, 2, D), 0.02),
        "ln_b": nrm(ks[5], (DEPTH, 2, D), 0.02),
        "gla_w_in": nrm(ks[6], (N_GLA_LAYERS, D, GLA_IN_WIDTH), D ** -0.5),
        "gla_w_gk2": nrm(ks[7], (N_GLA_LAYERS, GLA_GATE_RANK, GLA_DK), GLA_GATE_RANK ** -0.5),
        "gla_b_gk": nrm(ks[8], (N_GLA_LAYERS, GLA_DK), 0.1),
        "gla_g_norm": 1.0 + nrm(ks[9], (N_GLA_LAYERS, GLA_HEADS, GLA_DV_HEAD), 0.02),
        "gla_w_out": nrm(ks[10], (N_GLA_LAYERS, GLA_DV, D), DEEPNORM_BETA * GLA_DV ** -0.5),
        "att_w_in": nrm(ks[11], (N_ATT_LAYERS, D, 3 * D), D ** -0.5),
        "att_b_in": nrm(ks[12], (N_ATT_LAYERS, 3 * D), 0.02),
        "att_rel_bias": nrm(ks[13], (N_ATT_LAYERS, ATT_HEADS, N_REL), 0.2),
        "att_w_out": nrm(ks[14], (N_ATT_LAYERS, D, D), DEEPNORM_BETA * D ** -0.5),
        "ff_w1": nrm(jax.random.fold_in(ks[15], 0), (DEPTH, D, D_FF), D ** -0.5),
        "ff_w2": nrm(jax.random.fold_in(ks[15], 1), (DEPTH, D_FF, D), DEEPNORM_BETA * D_FF ** -0.5),
    }

def second_block(x, c, w_ada, b_ada, ln_g, ln_b, gla_w_in, gla_w_gk2, gla_b_gk, gla_g_norm, gla_w_out,
              att_w_in, att_b_in, att_rel_bias, att_w_out, ff_w1, ff_w2):
    c_act = jax.nn.silu(c)
    for i in range(DEPTH):
        mods = jnp.split(c_act @ w_ada[i] + b_ada[i], 6, axis=-1)
        sh1, sc1, g1, sh2, sc2, g2 = [m[:, None, :] for m in mods]
        u = x * (1.0 + sc1) + sh1
        j = i // N_MIXERS_2
        if i % N_MIXERS_2 == 0:
            y = gla_mixer(u, gla_w_in[j], gla_w_gk2[j], gla_b_gk[j], gla_g_norm[j], gla_w_out[j])
        else:
            y = chunk_attention(u, att_w_in[j], att_b_in[j], att_rel_bias[j], att_w_out[j])
        x = layer_norm_2(DEEPNORM_ALPHA * x + (1.0 + g1) * y, ln_g[i, 0], ln_b[i, 0])
        u = x * (1.0 + sc2) + sh2
        y = squared_relu_mlp(u, ff_w1[i], ff_w2[i])
        x = layer_norm_2(DEEPNORM_ALPHA * x + (1.0 + g2) * y, ln_g[i, 1], ln_b[i, 1])
    return x


def setup_inputs(seed=0):
    out = dict(first_inputs(seed))
    for name, value in second_inputs(seed + 1).items():
        if name != "x":
            out[name + "_2"] = value
    return out


def reference(
    x, pre_norm_g, w_in, mla_q_norm_g, mla_w_uq, mla_kv_norm_g, mla_w_ukv, rel_bias, conv_dw_w,
    conv_dw_b, conv_ln_g, conv_ln_b, conv_pw_w, conv_pw_b, w_out, post_norm_g, c_2, w_ada_2,
    b_ada_2, ln_g_2, ln_b_2, gla_w_in_2, gla_w_gk2_2, gla_b_gk_2, gla_g_norm_2, gla_w_out_2,
    att_w_in_2, att_b_in_2, att_rel_bias_2, att_w_out_2, ff_w1_2, ff_w2_2,
):
    x = first_block(
        x, pre_norm_g, w_in, mla_q_norm_g, mla_w_uq, mla_kv_norm_g, mla_w_ukv, rel_bias,
        conv_dw_w, conv_dw_b, conv_ln_g, conv_ln_b, conv_pw_w, conv_pw_b, w_out, post_norm_g,
    )
    return second_block(
        x, c_2, w_ada_2, b_ada_2, ln_g_2, ln_b_2, gla_w_in_2, gla_w_gk2_2, gla_b_gk_2,
        gla_g_norm_2, gla_w_out_2, att_w_in_2, att_b_in_2, att_rel_bias_2, att_w_out_2, ff_w1_2,
        ff_w2_2,
    )


_drawn_inputs = setup_inputs


def setup_inputs(seed=0):
    import zlib

    import numpy as np

    out = dict(_drawn_inputs(seed))
    spreads = {}
    factors = {'mla_q_norm_g': 5.222,
     'mla_kv_norm_g': 2.984,
     'conv_ln_b': 3.386,
     'gla_b_gk_2': 7.111,
     'gla_g_norm_2': 23.59,
     'att_b_in_2': 7.52,
     'att_rel_bias_2': 5.903}
    for name, (base, spread) in spreads.items():
        noise = np.random.default_rng([zlib.crc32(name.encode()), seed]).standard_normal(out[name].shape)
        drawn = base * np.exp(spread * noise) if base else spread * noise
        out[name] = __import__('jax').numpy.asarray(drawn.astype(out[name].dtype))
    for name, factor in factors.items():
        out[name] = (out[name] * factor).astype(out[name].dtype)
    return out
```

```python
from contextlib import ExitStack
import math

import concourse.bass as bass
from concourse import mybir
import numpy as np

F32 = mybir.dt.float32
U32 = mybir.dt.uint32
I32 = mybir.dt.int32
ALU = mybir.AluOpType
ACT = mybir.ActivationFunctionType

P = 128
S = 256
NT = S // P
D = 1024
KC = D // P
DEPTH = 2
EPS = 1e-6
ROOT_GUESS = 0x5F3759DF
H = 4
HD = 64
QR, KVR, RD = 192, 128, 32
MLA_IN = QR + KVR + RD
QD = HD + RD
MLA_SCALE = float(QD) ** -0.5
HD_SCALE = float(HD) ** -0.5
GW = H * HD
TAPS = 31
NB = 32
NEG = -3.0e38

UNIT = 2048
SLOTS = 3
W1 = 18
A1 = 12
U1 = W1 + A1
T1 = U1 // SLOTS

W_AT = [5 * (w // 3) + (0, 1, 3)[w % 3] for w in range(W1)]
A_AT = [5 * (a // 2) + (2, 4)[a % 2] for a in range(A1)]
(U_MLA0, U_MLA1, U_CA, U_CG, U_G0, U_G1, U_G2, U_G3, U_BQ, U_BK, U_V0, U_V1, U_CQ, U_CK,
 U_O0, U_O1, U_O2, U_O3) = W_AT

C_PRE, C_QG, C_KVG, C_DWW, C_DWB, C_LNG, C_LNB, C_PWB = 0, 8, 10, 11, 73, 75, 77, 79
NCOL = 81
M_UQ, M_UKV, M_PW = 0, 768, 1280
NSMALL = 1792
K_ID, K_CAUSAL, K_KEEP, K_UNEG, K_ONEG, K_ROPE = 0, 128, 384, 512, 640, 768
K_ONE, K_CUM, K_LOW, K_UP = 832, 960, 1088, 1216
NCONST = 1344

CHUNK = 64
GLA = 512
GLA_SCALE = float(GLA // H) ** -0.5
ALPHA = (2.0 * DEPTH) ** 0.25
LN_EPS = 1e-5
ATT_H = 16
GROUPS = 16
B_ADA, B_LNG, B_LNB, B_GN, B_QK = 0, 64, 88, 112, 120
NCOLB = 136
ARENA = 25200

AG = 9
NG = 16 + AG
N_GLA = DEPTH * U1
N_FF0 = N_GLA + NG
N_ATT = N_FF0 + 2 * GROUPS + 15
N_FF1 = N_ATT + 16
GW_AT = [w + w // 2 for w in range(16)]
GA_AT = [3 * a + 2 for a in range(AG - 1)] + [NG - 1]
RE = 4 * DEPTH
HE = 8 * DEPTH

ACT_STEPS, DVE_STEPS, ATT_STEPS = 20, 184, 20


class Event:

    def __init__(self, sem, per):
        self.sem, self.per = sem, per

    def at(self, layer, k):
        return layer * self.per + k if self.per else k


class Chain:

    def __init__(self, eng, sem):
        self.eng, self.sem, self.base, self.n = eng, sem, 0, 0

    def enter(self, turn, per):
        self.start, self.per = self.base + self.n, per
        self.base, self.n = self.start + turn * per, 0

    def leave(self, turns):
        assert self.n == self.per, ("steps in the loop", self.n)
        self.base, self.n = self.start + turns * self.per, 0

    def do(self, ins):
        ins.then_inc(self.sem, 1)
        self.n += 1

    def pass_waits(self):
        self.eng.sem_inc(self.sem, 1)
        self.n += 1

    def sync(self, back=0):
        self.eng.wait_ge(self.sem, self.base + self.n - back)


def build(nc, x, units, cols, small, post_g, consts, onehot, rel_bias, ccol, colb_in, ada_rows,
          ln_rows, low_in, gk_in, att_line, v_row, out):
    with ExitStack() as ctx:
        def sb(name, shape, dt=F32):
            return ctx.enter_context(nc.sbuf_tensor(name, shape, dt))

        def sem(name):
            return ctx.enter_context(nc.semaphore(name))

        def event(name, per):
            return Event(sem(name), per)

        bank = [ctx.enter_context(nc.psum_tensor(f"bank{i}", [P, 512], F32)) for i in range(8)]
        G, A = bank[:4], bank[4:]
        ZB = ((G[2], 0, 512), (G[3], 512, 512), (A[0], 1024, 256), (A[1], 1280, 256))
        ZPOS = (0, 2, 1, 3)

        zeros = sb("zeros", [P, 512], mybir.dt.bfloat16)
        raw = sb("raw", [P, SLOTS, UNIT])
        xt = sb("xt", [P, NT, D])
        xs = sb("xs", [P, NT, D])
        hT = sb("hT", [P, KC, S])
        gateT = sb("gateT", [P, KC, S])
        yT = sb("yT", [P, KC, S])
        ada = sb("ada", [P, 6 * D])
        kst = sb("kst", [P, NCONST])
        ident = kst[:, K_ID:K_ID + P]
        causal = kst[:, K_CAUSAL:K_CAUSAL + S]
        keep = kst[:, K_KEEP:K_KEEP + P]
        uneg = kst[:, K_UNEG:K_UNEG + P]
        oneg = kst[:, K_ONEG:K_ONEG + P]
        ones = kst[:, K_ONE:K_ONE + P]
        cummat = kst[:, K_CUM:K_CUM + P]
        lower = kst[:, K_LOW:K_LOW + P].bitcast(U32)
        upper = kst[:, K_UP:K_UP + P].bitcast(U32)
        rope = kst[:, K_ROPE:K_ROPE + 64].rearrange("p (t c i) -> p t c i", t=NT, c=2)
        oneh = sb("oneh", [NB + 1, 384])
        relb = sb("relb", [NB + 1, H])
        rr = sb("rr", [H, 384])
        cact = sb("cact", [P, KC])
        ss = sb("ss", [P, 8])
        ms = sb("ms", [P, 8])
        r0 = sb("r0", [P, 8])
        guess = sb("guess", [P, 8], I32)
        nt0 = sb("nt0", [P, 8])
        nt1 = sb("nt1", [P, 8])
        rs = sb("rs", [P, 8])
        probs = sb("probs", [P, 2, 384])
        probsT = sb("probsT", [P, 2, 384])
        mx = sb("mx", [P, 2, 2])
        nm = sb("nm", [P, 2, 2])
        rsum = sb("rsum", [P, 2, 2])
        rinv = sb("rinv", [P, 2, 2])
        bst = sb("bst", [P, NT, 12])
        bag = sb("bag", [P, NT, 2])
        colb = sb("colb", [P, NCOLB])
        wlow = sb("wlow", [P, KC, 16])
        wgk = sb("wgk", [17, GLA])
        arena = sb("arena", [P, ARENA])

        def views(offset=0):
            at = [offset]

            def view(*dims):
                n = math.prod(dims)
                assert at[0] + n <= ARENA, "the arena is full"
                v = arena[:, at[0]:at[0] + n]
                at[0] += n
                names = "abcd"[:len(dims)]
                if len(dims) == 1:
                    return v
                return v.rearrange(f"p ({' '.join(names)}) -> p {' '.join(names)}", **dict(zip(names, dims)))

            return view

        view1 = views()
        col = view1(NCOL)
        sm = view1(NSMALL)
        gb = view1(D)
        zline = view1(H, S)
        moba_bias = view1(H, S)
        mu = view1(NT, MLA_IN)
        cn = view1(NT, QR + KVR)
        cT = view1(3, S)
        qn = view1(NT, H, QD)
        kn = view1(NT, H, QD)
        va = view1(NT, H, HD)
        qT = view1(H, S)
        kT = view1(H, S)
        rt = view1(4, NT, H, 16)
        qkB = view1(2, 2, S)
        qkC = view1(2, 2, S)
        vBC = view1(NT, 2 * GW)
        spl = view1(1536)
        lbeta = view1(1536)
        nl = view1(1536)
        th = view1(2, S)
        xg = view1(2, TAPS - 1 + S)
        cacc = view1(2, S)
        cnat = view1(NT, GW)
        zT = view1(2, S)
        view2 = views()
        gate_row = view2(DEPTH, 2, D)
        ln_row = view2(2, D)
        shsc = view2(4 * KC)
        ucoef = view2(4, 2, KC)
        ytmp = view2(NT, D)
        stay = 4 * D + 2 * D + 4 * KC + 8 * KC + NT * D
        view3 = views(stay)
        low = view3(S)
        la = view3(NT, GLA)
        las = view3(NT, GLA)
        cum = view3(H, S)
        epos, eneg, eend = view3(H, S), view3(H, S), view3(H, S)
        qf, qb, kf, kb, ke = (view3(H, S) for _ in range(5))
        ken = view3(NT, H, P)
        vg = yT.rearrange("p k s -> p (k s)").rearrange("p (t d) -> p t d", t=NT)
        att = view3(H, NT, P)
        state = view3(3, H, S)
        view4 = views(stay)
        relu = view4(3, 2, S)
        hid = view4(3, 2, S)
        tbias = view4(ATT_H, S)
        tline = view4(ATT_H, S)
        tcur = view4(H, S)
        vrow = view4(D)
        vcur = view4(GW)
        bcur = view4(4)
        qk4 = view4(2, 2, S)
        v4 = view4(NT, GW)
        rr_dram = nc.dram_tensor("rr_scratch", (H, 384), F32, kind="Internal").ap()

        landed = [sem(f"landed{i}") for i in range(SLOTS)]
        used = [sem(f"used{i}") for i in range(SLOTS)]
        x_in, const_in, rel_in, relb_in, line_in, bias_ready, rr_out, y_out = (sem(n) for n in (
            "x_in", "const_in", "rel_in", "relb_in", "line_in", "bias_ready", "rr_out", "y_out"))
        layer_in = event("layer_in", 48)
        act_step, dve_step = sem("act_step"), sem("dve_step")
        ones_ready, rr_psum, rr_ready, cact_ready = sem("ones_ready"), sem("rr_psum"), sem("rr_ready"), sem("cact_ready")
        x_new = event("x_new", 2)
        ss_ready = event("ss_ready", 1)
        ms_ready = event("ms_ready", 4)
        xs_ready = event("xs_ready", 2)
        htp_ready = event("htp_ready", 4)
        ht_act, ht_dve = event("ht_act", 4), event("ht_dve", 4)
        mu_ready = event("mu_ready", 2)
        ssm_ready = event("ssm_ready", 1)
        cn_ready = event("cn_ready", 4)
        cnp_ready = event("cnp_ready", 1)
        ct_ready = event("ct_ready", 3)
        th_ready = event("th_ready", 1)
        xg_ready = event("xg_ready", 1)
        silu_ready = event("silu_ready", 4)
        up_ready = event("up_ready", 2)
        upc_ready = event("upc_ready", 6)
        qk_ready = event("qk_ready", 4)
        v_ready = event("v_ready", 2)
        z_ready = event("z_ready", 2)
        spl_ready = event("spl_ready", 1)
        nl_ready = event("nl_ready", 3)
        sfx_ready = event("sfx_ready", 3)
        lbs_ready = event("lbs_ready", 3)
        ex_ready = event("ex_ready", 1)
        at_ready = event("at_ready", 2)
        rope_ready = event("rope_ready", 4)
        qkp_ready = event("qkp_ready", 4)
        qkT_ready = event("qkT_ready", 4)
        score_ready, nm_ready, exp_ready, pn_ready = (event(n, 8) for n in (
            "score_ready", "nm_ready", "exp_ready", "pn_ready"))
        ptp_ready, pt_ready, pv_ready = (event(n, 8) for n in ("ptp_ready", "pt_ready", "pv_ready"))
        osb_ready = event("osb_ready", 1)
        y_ready = event("y_ready", 5)
        conv_ready = event("conv_ready", 2)
        cvp_ready = event("cvp_ready", 3)
        cnat_ready = event("cnat_ready", 2)
        z_conv = event("z_conv", 2)
        sso_ready = event("sso_ready", 1)
        zeros_ready, low_ones, att_zero = sem("zeros_ready"), sem("low_ones"), sem("att_zero")
        colb_ready, gla_in, row_in, lnrow_in, line2_in = (sem(n) for n in (
            "colb_ready", "gla_in", "row_in", "lnrow_in", "line2_in"))
        tb_ready = event("tb_ready", 3)
        modc_psum, modr_psum = event("modc_psum", 1), event("modr_psum", 2)
        modc_used, coef_ready, gate_used = event("modc_used", 1), event("coef_ready", 1), event("gate_used", 2)
        tp_ready = event("tp_ready", 4)
        u_act, u_dve = event("u_act", 4), event("u_dve", 4)
        xm_ready = event("xm_ready", 1)
        y_half = event("y_half", 1)
        xn_ready, xu_ready = event("xn_ready", 2), event("xu_ready", 1)
        lowp_ready, low_ready, lgp_ready, las_ready = (sem(n) for n in ("lowp_ready", "low_ready", "lgp_ready", "las_ready"))
        la_ready, cump_ready, cum_ready, decay_ready = (sem(n) for n in ("la_ready", "cump_ready", "cum_ready", "decay_ready"))
        qkm_ready, vg_ready, gate_ready = sem("qkm_ready"), sem("vg_ready"), sem("gate_ready")
        attp_ready, att_ready, kep_ready, ken_ready = (sem(n) for n in ("attp_ready", "att_ready", "kep_ready", "ken_ready"))
        stp_ready, st0_ready, st_ready = sem("stp_ready"), sem("st0_ready"), sem("st_ready")
        og_psum, og_sq, og_ready, ogp_ready, yg_ready = (sem(n) for n in (
            "og_psum", "og_sq", "og_ready", "ogp_ready", "yg_ready"))
        relu_ready, hid_ready = event("relu_ready", GROUPS), event("hid_ready", GROUPS)
        bc_ready, cur_ready = event("bc_ready", 1), event("cur_ready", 2)
        qa_ready, ka_ready = event("qa_ready", 2), event("ka_ready", 2)
        v4_ready, oq_ready = event("v4_ready", 2), event("oq_ready", 1)

        def wait_landed(eng, turns, n):
            eng.wait_ge(landed[n % SLOTS], 16 * (turns + n // SLOTS + 1))

        def wait_used(eng, turns, n):
            eng.wait_ge(used[n % SLOTS], turns + n // SLOTS + 1)

        N_UNITS = units.shape[0]
        block = ctx.enter_context(nc.Block())

        @block.sync
        def _(sp):
            sp.dma_start(xt[:], x.rearrange("a (t p) d -> p (a t) d", p=P)).then_inc(x_in, 16)
            sp.dma_start(kst[:], consts).then_inc(const_in, 16)
            sp.dma_start(oneh[:], onehot).then_inc(rel_in, 16)
            sp.dma_start(cact[:], ccol).then_inc(rel_in, 16)
            for s in range(SLOTS):
                sp.dma_start(raw[:, s, :], units[s, :, :]).then_inc(landed[s], 16)
            with sp.Fori(1, N_UNITS // SLOTS) as i:
                for s in range(SLOTS):
                    sp.wait_ge(used[s], i)
                    sp.dma_start(raw[:, s, :], units[i * SLOTS + s, :, :]).then_inc(landed[s], 16)
            sp.wait_ge(xu_ready.sem, xu_ready.at(3, 1))
            sp.dma_start(out.rearrange("a (t p) d -> p (a t) d", p=P), xt[:]).then_inc(y_out, 16)
            sp.wait_ge(y_out, 16)

        @block.gpsimd
        def _(pool):
            pool.memset(zeros[:], 0.0).then_inc(zeros_ready, 1)
            pool.memset(relb[:], 1.0).then_inc(ones_ready, 1)

            def layer_vectors(l):
                if l > 0:
                    pool.wait_ge(x_new.sem, x_new.at(l, 2))
                pool.dma_start(col[:], cols[l, :, :]).then_inc(layer_in.sem, 16)
                pool.dma_start(sm[:], small[l, :, :]).then_inc(layer_in.sem, 16)
                pool.dma_start(gb[:], post_g[l, :, :].to_broadcast([P, D])).then_inc(layer_in.sem, 16)

            pool.wait_ge(ones_ready, 1)
            pool.dma_start(relb[0:NB, :], rel_bias).then_inc(relb_in, 16)
            layer_vectors(0)
            pool.dma_start(colb[:], colb_in).then_inc(colb_ready, 16)
            pool.dma_start(wlow[:].rearrange("p k r -> p (k r)"), low_in).then_inc(gla_in, 16)
            pool.dma_start(wgk[0:17, :], gk_in).then_inc(gla_in, 16)
            pool.wait_ge(rr_ready, 1)
            pool.dma_start(rr_dram, rr[:]).then_inc(rr_out, 16)
            pool.wait_ge(rr_out, 16)
            pool.dma_start(zline[:], bass.AP(rr_dram.tensor, 0, [[1, P], [384, H], [1, S]])).then_inc(line_in, 16)
            pool.wait_ge(line_in, 16)
            pool.tensor_copy(moba_bias[:], zline[:, :, ::-1]).then_inc(bias_ready, 1)
            for l in range(1, DEPTH):
                layer_vectors(l)
            pool.wait_ge(x_new.sem, 2 * DEPTH + 2)
            pool.dma_start(gate_row[:].rearrange("p l g d -> p (l g d)"), ada_rows.to_broadcast([P, 4 * D])).then_inc(row_in, 16)
            pool.dma_start(ln_row[:].rearrange("p g d -> p (g d)"), ln_rows[0, :, :].to_broadcast([P, 2 * D])).then_inc(lnrow_in, 16)
            pool.memset(low[0:32, :], 1.0).then_inc(low_ones, 1)
            pool.memset(att[:], 0.0).then_inc(att_zero, 1)

            def x_update(s):
                pool.wait_ge(xn_ready.sem, xn_ready.at(s, 2))
                pool.wait_ge(lnrow_in, 16 * (s + 1))
                pool.tensor_tensor(xt[:], xs[:], ln_row[:, 0, :].unsqueeze(1).to_broadcast([P, NT, D]), ALU.mult).then_inc(xm_ready.sem, 1)
                pool.wait_ge(xm_ready.sem, s + 1)
                pool.tensor_tensor(xt[:], xt[:], ln_row[:, 1, :].unsqueeze(1).to_broadcast([P, NT, D]), ALU.add).then_inc(xu_ready.sem, 1)
                pool.wait_ge(xu_ready.sem, s + 1)
                pool.dma_start(ln_row[:].rearrange("p g d -> p (g d)"), ln_rows[s + 1, :, :].to_broadcast([P, 2 * D])).then_inc(lnrow_in, 16)

            x_update(0)
            pool.dma_start(tline[:], bass.AP(att_line.tensor, 0, [[1, P], [384, ATT_H], [1, S]])).then_inc(line2_in, 16)
            pool.dma_start(vrow[:], v_row.to_broadcast([P, D])).then_inc(line2_in, 16)
            pool.wait_ge(line2_in, 32)
            pool.tensor_copy(tbias[:], tline[:, :, ::-1]).then_inc(tb_ready.sem, 1)
            pool.wait_ge(tb_ready.sem, 1)
            pool.memset(tbias[0:CHUNK, :, S - CHUNK:], NEG).then_inc(tb_ready.sem, 1)
            x_update(1)
            pool.wait_ge(tb_ready.sem, 2)

            def projection_biases(qd):
                pool.tensor_copy(bcur[:], colb[:, bass.ds(B_QK + 4 * qd, 4)]).then_inc(bc_ready.sem, 1)

            def head_biases(qd):
                pool.tensor_copy(vcur[:], vrow[:, bass.ds(GW * qd, GW)]).then_inc(cur_ready.sem, 1)
                pool.tensor_copy(tcur[:], tbias[:, bass.ds(H * qd, H), :]).then_inc(cur_ready.sem, 1)

            projection_biases(0)
            head_biases(0)
            with pool.Fori(0, H - 1) as qd:
                pool.wait_ge(nm_ready.sem, HE + H * qd + 1)
                projection_biases(qd + 1)
                pool.wait_ge(nm_ready.sem, HE + H * qd + H)
                head_biases(qd + 1)
            x_update(2)

        @block.scalar
        def _(act):
            ch = Chain(act, act_step)

            def head_exp(h0, j, scale):
                b = j % 2
                act.wait_ge(nm_ready.sem, h0 + j + 1)
                ch.do(act.activation(probs[:, b, 0:P], probs[:, b, 0:P], ACT.Exp, scale=scale,
                                     bias=nm[:, b, 0:1], accum_out=rsum[:, b, 0:1]))
                act.activation(probs[:, b, P:384], probs[:, b, P:384], ACT.Exp, scale=scale,
                               bias=nm[:, b, 1:2], accum_out=rsum[:, b, 1:2]).then_inc(exp_ready.sem, 1)

            def head_copy(h0, j, banks, again=False):
                b = j % 2
                act.wait_ge(ptp_ready.sem, h0 + j + 1)
                if j >= 2 or again:
                    act.wait_ge(pv_ready.sem, h0 + j - 1)
                act.activation(probsT[:, b, :], banks[b][:, 0:384], ACT.Copy).then_inc(pt_ready.sem, 1)

            act.wait_ge(rel_in, 32)
            act.activation(cact[:], cact[:], ACT.Silu).then_inc(cact_ready, 1)
            act.wait_ge(x_in, 16)
            act.wait_ge(const_in, 16)
            with act.Fori(0, DEPTH) as l:
                ch.enter(l, ACT_STEPS)
                act.wait_ge(x_new.sem, x_new.at(l, 1))
                ch.do(act.activation(xs[:, 0, :], xt[:, 0, :], ACT.Square, accum_out=ss[:, 0:1]))
                act.wait_ge(x_new.sem, x_new.at(l, 2))
                act.activation(xs[:, 1, :], xt[:, 1, :], ACT.Square, accum_out=ss[:, 1:2]).then_inc(ss_ready.sem, 1)
                act.wait_ge(layer_in.sem, layer_in.at(l, 48))
                for q in range(2):
                    act.wait_ge(htp_ready.sem, htp_ready.at(l, q + 1))
                    for i in range(2):
                        c = 2 * q + i
                        act.activation(hT[:, c, :], G[q][:, i * S:(i + 1) * S], ACT.Copy,
                                       scale=col[:, C_PRE + c:C_PRE + c + 1]).then_inc(ht_act.sem, 1)
                wait_used(act, T1 * l, U_MLA1)
                for t in range(NT):
                    act.activation(mu[:, t, :], A[t][:, 0:MLA_IN], ACT.Copy).then_inc(mu_ready.sem, 1)
                act.wait_ge(mu_ready.sem, mu_ready.at(l, 2))
                for t in range(NT):
                    ch.do(act.activation(cn[:, t, 0:QR], mu[:, t, 0:QR], ACT.Square, accum_out=ss[:, t:t + 1]))
                    last = act.activation(cn[:, t, QR:], mu[:, t, QR:QR + KVR], ACT.Square,
                                          accum_out=ss[:, 2 + t:3 + t])
                    if t == 0:
                        ch.do(last)
                last.then_inc(ssm_ready.sem, 1)
                wait_used(act, T1 * l, U_CG)
                act.activation(th[:].rearrange("p c s -> p (c s)"), G[1][:], ACT.Tanh, scale=0.5).then_inc(th_ready.sem, 1)
                for g, u in enumerate((U_G0, U_G1)):
                    wait_used(act, T1 * l, u)
                    act.activation(gateT[:, 2 * g:2 * g + 2, :], G[2 + g][:], ACT.Silu).then_inc(silu_ready.sem, 1)
                act.wait_ge(cnp_ready.sem, cnp_ready.at(l, 1))
                act.activation(cT[:, 0, :], A[2][:, 0:S], ACT.Copy, scale=col[:, C_QG:C_QG + 1]).then_inc(ct_ready.sem, 1)
                act.activation(cT[:, 2, :], A[2][:, S:2 * S], ACT.Copy, scale=col[:, C_KVG:C_KVG + 1]).then_inc(ct_ready.sem, 1)
                act.activation(cT[0:64, 1, :], A[3][0:64, 0:S], ACT.Copy,
                               scale=col[0:64, C_QG + 1:C_QG + 2]).then_inc(ct_ready.sem, 1)
                for g, u in enumerate((U_G2, U_G3)):
                    wait_used(act, T1 * l, u)
                    act.activation(gateT[:, 4 + 2 * g:6 + 2 * g, :], G[g][:], ACT.Silu).then_inc(silu_ready.sem, 1)
                wait_used(act, T1 * l, U_BQ)
                act.activation(qkB[:, 0], G[2][:], ACT.Copy, scale=HD_SCALE).then_inc(qk_ready.sem, 1)
                wait_used(act, T1 * l, U_BK)
                act.activation(qkB[:, 1], G[3][:], ACT.Copy).then_inc(qk_ready.sem, 1)
                act.wait_ge(up_ready.sem, up_ready.at(l, 1))
                for t in range(NT):
                    act.activation(qn[:, t].rearrange("p h d -> p (h d)"), A[t][:, 0:H * QD], ACT.Copy).then_inc(upc_ready.sem, 1)
                act.wait_ge(up_ready.sem, up_ready.at(l, 2))
                for t in range(NT):
                    kv = A[2 + t][:].rearrange("p (h d) -> p h d", h=H)
                    act.activation(kn[:, t, :, 0:HD], kv[:, :, 0:HD], ACT.Copy).then_inc(upc_ready.sem, 1)
                    act.activation(va[:, t], kv[:, :, HD:], ACT.Copy).then_inc(upc_ready.sem, 1)
                wait_used(act, T1 * l, U_V1)
                for t in range(NT):
                    act.activation(vBC[:, t, :], G[t][:], ACT.Copy).then_inc(v_ready.sem, 1)
                act.wait_ge(z_ready.sem, z_ready.at(l, 2))
                for b, c0, w in ZB:
                    ch.do(act.activation(spl[:, c0:c0 + w], b[:, 0:w], ACT.Abs))
                ch.sync()
                ch.do(act.activation(spl[:], spl[:], ACT.Exp, scale=-1.0))
                ch.sync()
                act.activation(spl[:], spl[:], ACT.Ln, bias=1.0).then_inc(spl_ready.sem, 1)
                wait_used(act, T1 * l, U_CQ)
                act.activation(qkC[:, 0], G[0][:], ACT.Copy, scale=HD_SCALE).then_inc(qk_ready.sem, 1)
                wait_used(act, T1 * l, U_CK)
                act.activation(qkC[:, 1], G[1][:], ACT.Copy).then_inc(qk_ready.sem, 1)
                for i, (dst, h0, b) in enumerate(((qT, 0, A[2]), (qT, 2, A[3]), (kT, 0, A[1]), (kT, 2, A[2]))):
                    act.wait_ge(qkp_ready.sem, qkp_ready.at(l, i + 1))
                    act.activation(dst[0:QD, h0:h0 + 2, :], b[0:QD, :], ACT.Copy).then_inc(qkT_ready.sem, 1)
                act.wait_ge(lbs_ready.sem, lbs_ready.at(l, 3))
                act.activation(spl[:], lbeta[:], ACT.Exp).then_inc(ex_ready.sem, 1)
                for j in range(2 * H):
                    head_exp(8 * l, j, MLA_SCALE if j < H else 1.0)
                    if j >= 1:
                        head_copy(8 * l, j - 1, (A[3], A[0]))
                head_copy(8 * l, 2 * H - 1, (A[3], A[0]))
                act.wait_ge(cvp_ready.sem, cvp_ready.at(l, 2))
                for c in range(2):
                    act.activation(zT[:, c, :], G[2][:, c * S:(c + 1) * S], ACT.Silu,
                                   scale=col[:, C_LNG + c:C_LNG + c + 1],
                                   bias=col[:, C_LNB + c:C_LNB + c + 1]).then_inc(z_conv.sem, 1)
                for i, u in enumerate((U_O2, U_O3)):
                    wait_used(act, T1 * l, u)
                    for t in range(NT):
                        last = act.activation(xs[:, t, i * 512:(i + 1) * 512], G[2 * i + t][:], ACT.Square,
                                              accum_out=ss[:, 2 * i + t:2 * i + t + 1])
                        if 2 * i + t < 3:
                            ch.do(last)
                last.then_inc(sso_ready.sem, 1)
            ch.leave(DEPTH)

            def stage_input(s):
                act.wait_ge(coef_ready.sem, coef_ready.at(s // 2, 1))
                for q in range(2):
                    act.wait_ge(tp_ready.sem, tp_ready.at(s, q + 1))
                    for i in range(2):
                        c = 2 * q + i
                        act.activation(hT[:, c, :], G[q][:, i * S:(i + 1) * S], ACT.Identity,
                                       scale=ucoef[:, s, 0, c:c + 1], bias=ucoef[:, s, 1, c:c + 1]).then_inc(u_act.sem, 1)

            def relu_group(turns, n, k):
                wait_used(act, turns, n)
                act.activation(relu[:, k], A[k][:], ACT.Relu).then_inc(relu_ready.sem, 1)

            stage_input(0)
            act.wait_ge(lowp_ready, 1)
            act.wait_ge(low_ones, 1)
            act.activation(low[0:16, :], G[3][0:16, 0:S], ACT.Copy).then_inc(low_ready, 1)
            act.wait_ge(lgp_ready, 1)
            for t in range(NT):
                ch.do(act.activation(las[:, t, :], A[t][:], ACT.Abs))
            ch.sync()
            ch.do(act.activation(las[:], las[:], ACT.Exp, scale=-1.0))
            ch.sync()
            act.activation(las[:], las[:], ACT.Ln, bias=1.0).then_inc(las_ready, 1)
            act.wait_ge(cump_ready, 1)
            for g in range(2):
                act.activation(cum[:, 2 * g:2 * g + 2, :], A[g][:], ACT.Copy).then_inc(cum_ready, 1)
            act.wait_ge(cum_ready, 2)
            act.activation(epos[:], cum[:], ACT.Exp).then_inc(decay_ready, 1)
            act.activation(eneg[:], cum[:], ACT.Exp, scale=-1.0).then_inc(decay_ready, 1)
            for h in range(H):
                for c in range(S // CHUNK):
                    e = (c + 1) * CHUNK
                    act.activation(eend[:, h, e - CHUNK:e], cum[:, h, e - CHUNK:e], ACT.Exp, scale=-1.0,
                                   bias=cum[:, h, e - 1:e]).then_inc(decay_ready, 1)
            for c in range(2):
                wait_used(act, 0, N_GLA + GW_AT[5 + 2 * c])
                for t in range(NT):
                    act.activation(vg[:, t, c * 512:(c + 1) * 512], A[(2 + t, t)[c]][:], ACT.Copy).then_inc(vg_ready, 1)

            def gates(g0):
                for g in (g0, g0 + 1):
                    wait_used(act, 0, N_GLA + GW_AT[8 + g])
                    act.activation(gateT[:, 2 * g:2 * g + 2, :], G[g][:], ACT.Silu).then_inc(gate_ready, 1)

            gates(0)
            act.wait_ge(kep_ready, 1)
            for t in range(NT):
                act.activation(ken[:, t].rearrange("p h d -> p (h d)"), G[2 + t][:], ACT.Copy).then_inc(ken_ready, 1)
            act.wait_ge(stp_ready, 1)
            for g in range(2):
                act.activation(state[:, 0, 2 * g:2 * g + 2, :], G[g][:], ACT.Copy).then_inc(st0_ready, 1)
            for t in range(NT):
                act.wait_ge(og_psum, t + 1)
                for h in range(H):
                    act.activation(ytmp[:, t, h * S:(h + 1) * S], A[2 * t + h // 2][:, (h % 2) * S:(h % 2 + 1) * S],
                                   ACT.Square, accum_out=ss[:, 4 * t + h:4 * t + h + 1]).then_inc(og_sq, 1)
            gates(2)
            stage_input(1)
            relu_group(0, N_FF0, 0)
            with act.Fori(0, 5) as i:
                for k in range(3):
                    relu_group(3 * i, N_FF0 + 1 + 3 * k, (k + 1) % 3)
            stage_input(2)

            def keys(qd):
                act.wait_ge(bc_ready.sem, bc_ready.at(qd, 1))
                wait_used(act, qd, N_ATT + 1)
                for c in range(2):
                    act.activation(qk4[:, 1, c, :], G[1][:, c * S:(c + 1) * S], ACT.Identity, bias=bcur[:, 2 + c:3 + c],
                                   scale=1.0).then_inc(ka_ready.sem, 1)

            def four_heads(qd, more=True):
                h0 = HE + H * qd
                for j in range(H):
                    head_exp(h0, j, 1.0)
                    if j >= 1:
                        head_copy(h0, j - 1, (A[3], A[0]), True)
                if more:
                    keys(qd + 1)
                head_copy(h0, H - 1, (A[3], A[0]), True)

            keys(0)
            with act.Fori(0, H - 1) as qd:
                ch.enter(qd, H)
                four_heads(qd)
            ch.leave(H - 1)
            four_heads(H - 1, more=False)
            stage_input(3)
            relu_group(0, N_FF1, 0)
            with act.Fori(0, 5) as i:
                for k in range(3):
                    relu_group(2 * i, N_FF1 + 1 + 2 * k, (k + 1) % 3)

        @block.vector
        def _(dve):
            ch = Chain(dve, dve_step)

            def inv_root(v, n):
                dve.wait_ge(ms_ready.sem, v)
                bits = guess[:, 0:n]
                ch.do(dve.tensor_scalar(bits, ms[:, 0:n].bitcast(I32), 1, None, ALU.arith_shift_right))
                ch.sync()
                ch.do(dve.tensor_scalar(r0[:, 0:n].bitcast(I32), bits, -1, ROOT_GUESS, ALU.mult, ALU.add))
                for src, dst in ((r0, rs), (rs, r0), (r0, rs)):
                    ch.sync()
                    ch.do(dve.tensor_tensor(nt0[:, 0:n], src[:, 0:n], src[:, 0:n], ALU.mult))
                    ch.sync()
                    ch.do(dve.scalar_tensor_tensor(nt1[:, 0:n], nt0[:, 0:n], -0.5, ms[:, 0:n], ALU.mult, ALU.mult))
                    ch.sync()
                    ch.do(dve.scalar_tensor_tensor(dst[:, 0:n], nt1[:, 0:n], 1.5, src[:, 0:n], ALU.add, ALU.mult))
                ch.sync()

            def ada_unit(l, a):
                n, c0 = A_AT[a], 2 * (a % 4)
                wait_landed(dve, T1 * l, n)
                dst = ada[:, bass.ds((3 * l + a // 4) * D, D)]
                for i in range(2):
                    w = raw[:, n % SLOTS, i * D:(i + 1) * D]
                    cc = cact[:, c0 + i:c0 + i + 1]
                    if c0 + i == 0:
                        ins = dve.tensor_scalar(dst, w, cc, None, ALU.mult)
                    else:
                        if i == 0:
                            wait_used(dve, T1 * l, A_AT[a - 1])
                        ins = dve.scalar_tensor_tensor(dst, w, cc, dst, ALU.mult, ALU.add)
                    if i == 0:
                        ch.do(ins)
                        ch.sync()
                    else:
                        ins.then_inc(used[n % SLOTS], 1)

            def taps(j0, j1):
                for j in range(j0, j1):
                    for c in range(2):
                        w = col[:, C_DWW + 31 * c + j:C_DWW + 31 * c + j + 1]
                        if j == 0:
                            ins = dve.tensor_scalar(cacc[:, c, :], xg[:, c, 0:S], w,
                                                    col[:, C_DWB + c:C_DWB + c + 1], ALU.mult, ALU.add)
                        else:
                            ch.sync(1 if c == 0 or j0 < j < TAPS - 1 else 0)
                            ins = dve.scalar_tensor_tensor(cacc[:, c, :], xg[:, c, j:j + S], w, cacc[:, c, :],
                                                           ALU.mult, ALU.add)
                        if j < TAPS - 1:
                            ch.do(ins)
                        else:
                            ins.then_inc(conv_ready.sem, 1)

            def rotate(src, cs, sn, shape_h):
                lo, hi = (src[..., 0:16], src[..., 16:32])
                tmp = [rt[:, i, :, 0:shape_h, :] if shape_h > 1 else rt[:, i, :, 0, :] for i in range(4)]
                for i, (a, b) in enumerate(((lo, cs), (hi, sn), (lo, sn), (hi, cs))):
                    ch.do(dve.tensor_tensor(tmp[i], a, b, ALU.mult))
                ch.sync()
                return tmp

            def head_max(h0, j, banks, bias, scale, again=False):
                b = j % 2
                dve.wait_ge(score_ready.sem, h0 + j + 1)
                if j >= 2 or again:
                    dve.wait_ge(ptp_ready.sem, h0 + j - 1)
                ch.pass_waits()
                ch.do(dve.tensor_tensor_reduce(out=probs[:, b, 0:P], in0=banks[b][:, 0:P], in1=bias[:, P:2 * P],
                                               scale=1.0, scalar=NEG, op0=ALU.add, op1=ALU.max,
                                               accum_out=mx[:, b, 0:1]))
                ch.do(dve.tensor_tensor_reduce(out=probs[:, b, P:384], in0=banks[b][:, P:384], in1=bias,
                                               scale=1.0, scalar=NEG, op0=ALU.add, op1=ALU.max,
                                               accum_out=mx[:, b, 1:2]))
                ch.sync()
                dve.tensor_scalar(nm[:, b, :], mx[:, b, :], -scale, None, ALU.mult).then_inc(nm_ready.sem, 1)

            def head_norm(h0, j):
                b = j % 2
                dve.wait_ge(exp_ready.sem, h0 + j + 1)
                ch.do(dve.reciprocal(rinv[:, b, :], rsum[:, b, :]))
                ch.sync()
                ch.do(dve.tensor_scalar(probs[:, b, 0:P], probs[:, b, 0:P], rinv[:, b, 0:1], None, ALU.mult))
                dve.tensor_scalar(probs[:, b, P:384], probs[:, b, P:384], rinv[:, b, 1:2], None,
                                  ALU.mult).then_inc(pn_ready.sem, 1)

            dve.wait_ge(rr_psum, 1)
            dve.wait_ge(rel_in, 32)
            dve.tensor_copy(rr[:], G[0][0:H, 0:384]).then_inc(rr_ready, 1)
            dve.wait_ge(cact_ready, 1)
            dve.memset(xg[:, :, 0:TAPS - 1], 0.0).then_inc(x_new.sem, 2)
            dve.wait_ge(x_in, 16)
            dve.wait_ge(const_in, 16)
            with dve.Fori(0, DEPTH) as l:
                ch.enter(l, DVE_STEPS)
                dve.wait_ge(ss_ready.sem, ss_ready.at(l, 1))
                dve.tensor_scalar(ms[:, 0:2], ss[:, 0:2], 1.0 / D, EPS, ALU.mult, ALU.add).then_inc(ms_ready.sem, 1)
                inv_root(4 * l + 1, 2)
                for t in range(NT):
                    dve.tensor_scalar(xs[:, t, :], xt[:, t, :], rs[:, t:t + 1], None, ALU.mult).then_inc(xs_ready.sem, 1)
                dve.wait_ge(layer_in.sem, layer_in.at(l, 48))
                for q in range(2, 4):
                    dve.wait_ge(htp_ready.sem, htp_ready.at(l, q + 1))
                    for i in range(2):
                        c = 2 * q + i
                        dve.tensor_scalar(hT[:, c, :], G[q][:, i * S:(i + 1) * S],
                                          col[:, C_PRE + c:C_PRE + c + 1], None, ALU.mult).then_inc(ht_dve.sem, 1)
                ada_unit(l, 0)
                dve.wait_ge(ssm_ready.sem, ssm_ready.at(l, 1))
                ch.do(dve.tensor_scalar(ms[:, 0:2], ss[:, 0:2], 1.0 / QR, EPS, ALU.mult, ALU.add))
                dve.tensor_scalar(ms[:, 2:4], ss[:, 2:4], 1.0 / KVR, EPS, ALU.mult, ALU.add).then_inc(ms_ready.sem, 1)
                ada_unit(l, 1)
                inv_root(4 * l + 2, 4)
                for t in range(NT):
                    dve.tensor_scalar(cn[:, t, 0:QR], mu[:, t, 0:QR], rs[:, t:t + 1], None, ALU.mult).then_inc(cn_ready.sem, 1)
                    dve.tensor_scalar(cn[:, t, QR:], mu[:, t, QR:QR + KVR], rs[:, 2 + t:3 + t], None,
                                      ALU.mult).then_inc(cn_ready.sem, 1)
                kr = mu[:, :, QR + KVR:MLA_IN]
                tmp = rotate(kr, rope[:, :, 0, :], rope[:, :, 1, :], 1)
                for i, op in enumerate((ALU.subtract, ALU.add)):
                    dve.tensor_tensor(kn[:, :, :, HD + 16 * i:HD + 16 * (i + 1)],
                                      tmp[2 * i].unsqueeze(2).to_broadcast([P, NT, H, 16]),
                                      tmp[2 * i + 1].unsqueeze(2).to_broadcast([P, NT, H, 16]), op).then_inc(rope_ready.sem, 1)
                ada_unit(l, 2)
                dve.wait_ge(th_ready.sem, th_ready.at(l, 1))
                ch.do(dve.tensor_scalar(th[:], th[:], 0.5, 0.5, ALU.mult, ALU.add))
                ch.sync()
                dve.tensor_tensor(xg[:, :, TAPS - 1:], th[:], G[0][:].rearrange("p (c s) -> p c s", c=2),
                                  ALU.mult).then_inc(xg_ready.sem, 1)
                ada_unit(l, 3)
                dve.wait_ge(xg_ready.sem, xg_ready.at(l, 1))
                taps(0, 12)
                ada_unit(l, 4)
                taps(12, 20)
                ada_unit(l, 5)
                dve.wait_ge(upc_ready.sem, upc_ready.at(l, 2))
                dve.wait_ge(rope_ready.sem, rope_ready.at(l, 2))
                qr = qn[:, :, :, HD:]
                cs = rope[:, :, 0, :].unsqueeze(2).to_broadcast([P, NT, H, 16])
                sn = rope[:, :, 1, :].unsqueeze(2).to_broadcast([P, NT, H, 16])
                tmp = rotate(qr, cs, sn, H)
                for i, op in enumerate((ALU.subtract, ALU.add)):
                    dve.tensor_tensor(qn[:, :, :, HD + 16 * i:HD + 16 * (i + 1)], tmp[2 * i], tmp[2 * i + 1],
                                      op).then_inc(rope_ready.sem, 1)
                ada_unit(l, 6)
                taps(20, TAPS)
                ada_unit(l, 7)
                dve.wait_ge(spl_ready.sem, spl_ready.at(l, 1))
                for b, c0, w in ZB:
                    c = slice(c0, c0 + w)
                    ch.do(dve.scalar_tensor_tensor(lbeta[:, c], b[:, 0:w], 0.0, spl[:, c], ALU.min, ALU.subtract))
                    ch.do(dve.scalar_tensor_tensor(nl[:, c], b[:, 0:w], 0.0, spl[:, c], ALU.max, ALU.add))
                ch.sync()
                for i in range(3):
                    v = (nl[:, 512 * i:512 * (i + 1)].rearrange("p (h q) -> p h q", h=2)[:, :, 0:P] if i < 2
                         else nl[:, 1024:1536].rearrange("p (h q) -> p h q", h=H))
                    nh = 2 if i < 2 else H
                    dve.tensor_tensor(v, v, keep.unsqueeze(1).to_broadcast([P, nh, P]), ALU.mult).then_inc(nl_ready.sem, 1)
                ada_unit(l, 8)
                for i, b in enumerate((G[2], G[3], A[0])):
                    c = slice(512 * i, 512 * (i + 1))
                    dve.wait_ge(sfx_ready.sem, sfx_ready.at(l, i + 1))
                    dve.tensor_tensor(lbeta[:, c], b[:], lbeta[:, c], ALU.add).then_inc(lbs_ready.sem, 1)
                ada_unit(l, 9)
                dve.wait_ge(ex_ready.sem, ex_ready.at(l, 1))
                v0 = spl[:, 0:1024].rearrange("p (h q) -> p h q", h=H)[:, :, 0:P]
                v1 = spl[:, 1024:1536].rearrange("p (h q) -> p h q", h=H)
                for v in (v0, v1):
                    dve.tensor_tensor(v, v, keep.unsqueeze(1).to_broadcast([P, H, P]), ALU.mult).then_inc(at_ready.sem, 1)
                dve.wait_ge(bias_ready, 1)
                for j in range(2 * H):
                    head_max(8 * l, j, (A[1], A[2]), causal if j < H else moba_bias[:, j - H, :],
                             MLA_SCALE if j < H else 1.0)
                    if j >= 1:
                        head_norm(8 * l, j - 1)
                    if j == 1:
                        dve.wait_ge(cvp_ready.sem, cvp_ready.at(l, 1))
                        for t in range(NT):
                            ch.do(dve.bn_stats(bst[:, t, 0:6], G[2][:, t * GW:(t + 1) * GW]))
                        ch.sync()
                        ch.pass_waits()
                        for t in range(NT):
                            ch.do(dve.bn_aggr(bag[:, t, :], bst[:, t, 0:6]))
                        ch.sync()
                        dve.tensor_scalar(ms[:, 0:2], bag[:, :, 1], EPS, None, ALU.add).then_inc(ms_ready.sem, 1)
                    if j == 3:
                        inv_root(4 * l + 3, 2)
                        for t in range(NT):
                            dve.tensor_scalar(cnat[:, t, :], G[2][:, t * GW:(t + 1) * GW], bag[:, t, 0:1],
                                              rs[:, t:t + 1], ALU.subtract, ALU.mult).then_inc(cnat_ready.sem, 1)
                    if j == 4:
                        dve.wait_ge(osb_ready.sem, osb_ready.at(l, 1))
                        dve.tensor_tensor(yT[:, 2:4, :], gateT[:, 2:4, :],
                                          G[1][:].rearrange("p (c s) -> p c s", c=2), ALU.mult).then_inc(y_ready.sem, 1)
                    if j == 6:
                        dve.wait_ge(pv_ready.sem, pv_ready.at(l, H))
                        dve.tensor_tensor(yT[:, 0:2, :], gateT[:, 0:2, :],
                                          G[0][:].rearrange("p (c s) -> p c s", c=2), ALU.mult).then_inc(y_ready.sem, 1)
                head_norm(8 * l, 2 * H - 1)
                dve.wait_ge(cvp_ready.sem, cvp_ready.at(l, 3))
                for c in range(2):
                    dve.scalar_tensor_tensor(yT[:, 6 + c, :], G[2][:, c * S:(c + 1) * S],
                                             col[:, C_PWB + c:C_PWB + c + 1], gateT[:, 6 + c, :],
                                             ALU.add, ALU.mult).then_inc(y_ready.sem, 1)
                dve.wait_ge(pv_ready.sem, pv_ready.at(l, 2 * H))
                dve.tensor_tensor(yT[:, 4:6, :], gateT[:, 4:6, :],
                                  G[3][:].rearrange("p (c s) -> p c s", c=2), ALU.mult).then_inc(y_ready.sem, 1)
                ada_unit(l, 10)
                ada_unit(l, 11)
                dve.wait_ge(sso_ready.sem, sso_ready.at(l, 1))
                ch.do(dve.tensor_tensor(nt0[:, 0:2], ss[:, 0:2], ss[:, 2:4], ALU.add))
                ch.sync()
                dve.tensor_scalar(ms[:, 0:2], nt0[:, 0:2], 1.0 / D, EPS, ALU.mult, ALU.add).then_inc(ms_ready.sem, 1)
                inv_root(4 * l + 4, 2)
                for t in range(NT):
                    for i in range(2):
                        ch.do(dve.scalar_tensor_tensor(xs[:, t, i * 512:(i + 1) * 512], G[2 * i + t][:],
                                                       rs[:, t:t + 1], gb[:, i * 512:(i + 1) * 512],
                                                       ALU.mult, ALU.mult))
                    ch.sync()
                    dve.tensor_tensor(xt[:, t, :], xt[:, t, :], xs[:, t, :], ALU.add).then_inc(x_new.sem, 1)
            ch.leave(DEPTH)

            def coefficients(lay):
                dve.wait_ge(modc_psum.sem, modc_psum.at(lay, 1))
                dve.wait_ge(colb_ready, 16)
                dve.tensor_tensor(shsc[:], A[0][:, 0:4 * KC], colb[:, B_ADA + 32 * lay:B_ADA + 32 * (lay + 1)],
                                  ALU.add).then_inc(modc_used.sem, 1)
                dve.wait_ge(modc_used.sem, modc_used.at(lay, 1))
                for i in range(2):
                    s = 2 * lay + i
                    sh, sc = shsc[:, 16 * i:16 * i + 8], shsc[:, 16 * i + 8:16 * i + 16]
                    if s == 0:
                        ch.do(dve.tensor_scalar(ucoef[:, s, 0, :], sc, 1.0, None, ALU.add))
                        ch.do(dve.tensor_scalar(ucoef[:, s, 1, :], sh, 1.0, None, ALU.mult))
                    else:
                        g, b = (colb[:, c + 8 * (s - 1):c + 8 * s] for c in (B_LNG, B_LNB))
                        ch.do(dve.scalar_tensor_tensor(ucoef[:, s, 0, :], sc, 1.0, g, ALU.add, ALU.mult))
                        tmp = (nt0, nt1)[i]
                        ch.do(dve.scalar_tensor_tensor(tmp[:], sc, 1.0, b, ALU.add, ALU.mult))
                        ch.sync()
                        ch.do(dve.tensor_tensor(ucoef[:, s, 1, :], tmp[:], sh, ALU.add))
                ch.sync()
                dve.sem_inc(coef_ready.sem, 1)

            def gate_rows(lay):
                dve.wait_ge(row_in, 16)
                for r, (g, h, b) in enumerate(((0, 0, A[1]), (0, 1, A[2]), (1, 0, A[3]), (1, 1, A[0]))):
                    dve.wait_ge(modr_psum.sem, modr_psum.at(lay, 1 + r // 3))
                    row = gate_row[:, lay, g, h * 512:(h + 1) * 512]
                    ins = dve.scalar_tensor_tensor(row, b[:], 1.0, row, ALU.add, ALU.add)
                    if r % 2:
                        ins.then_inc(gate_used.sem, 1)
                    else:
                        ch.do(ins)

            def stage_input(s):
                for q in range(2, 4):
                    dve.wait_ge(tp_ready.sem, tp_ready.at(s, q + 1))
                    for i in range(2):
                        c = 2 * q + i
                        dve.tensor_scalar(hT[:, c, :], G[q][:, i * S:(i + 1) * S], ucoef[:, s, 0, c:c + 1],
                                          ucoef[:, s, 1, c:c + 1], ALU.mult, ALU.add).then_inc(u_dve.sem, 1)

            def ada_unit_1(turns, n, idx):
                wait_landed(dve, turns, n)
                dst = ada[:, bass.ds(idx * 256, 256)]
                for k in range(KC):
                    w = raw[:, n % SLOTS, k * 256:(k + 1) * 256]
                    if k == 0:
                        ins = dve.tensor_scalar(dst, w, cact[:, 0:1], None, ALU.mult)
                    else:
                        ch.sync()
                        ins = dve.scalar_tensor_tensor(dst, w, cact[:, k:k + 1], dst, ALU.mult, ALU.add)
                    if k < KC - 1:
                        ch.do(ins)
                    else:
                        ins.then_inc(used[n % SLOTS], 1)

            def deep_norm(s, first, last):
                lay, g = s // 2, s % 2
                dve.wait_ge(gate_used.sem, gate_used.at(lay, g + 1))
                if s > 0:
                    dve.wait_ge(xu_ready.sem, xu_ready.at(s - 1, 1))
                for h in range(2):
                    if h == 1:
                        wait_used(dve, 0, last)
                    elif first is not None:
                        wait_used(dve, 0, first)
                    else:
                        dve.wait_ge(y_half.sem, y_half.at(lay, 1))
                    c = slice(h * 512, (h + 1) * 512)
                    for t in range(NT):
                        ch.do(dve.tensor_tensor(ytmp[:, t, c], G[2 * h + t][:], gate_row[:, lay, g, c], ALU.mult))
                    for t in range(NT):
                        ch.sync(1)
                        ch.do(dve.scalar_tensor_tensor(xt[:, t, c], xt[:, t, c], ALPHA, ytmp[:, t, c], ALU.mult, ALU.add))
                    for t in range(NT):
                        ch.sync(1)
                        ch.do(dve.bn_stats(bst[:, t, 6 * h:6 * h + 6], xt[:, t, c]))
                ch.sync()
                ch.pass_waits()
                for t in range(NT):
                    ch.do(dve.bn_aggr(bag[:, t, :], bst[:, t, :]))
                ch.sync()
                dve.tensor_scalar(ms[:, 0:2], bag[:, :, 1], LN_EPS, None, ALU.add).then_inc(ms_ready.sem, 1)
                inv_root(RE + 2 + s, 2)
                for t in range(NT):
                    dve.tensor_scalar(xs[:, t, :], xt[:, t, :], bag[:, t, 0:1], rs[:, t:t + 1], ALU.subtract,
                                      ALU.mult).then_inc(xn_ready.sem, 1)

            def square(s, g, k):
                dve.wait_ge(relu_ready.sem, relu_ready.at(s // 2, g + 1))
                dve.tensor_tensor(hid[:, k], relu[:, k], relu[:, k], ALU.mult).then_inc(hid_ready.sem, 1)

            coefficients(0)
            stage_input(0)
            gate_rows(0)
            ada_unit_1(0, N_GLA + GA_AT[0], 0)
            dve.wait_ge(las_ready, 1)
            for t in range(NT):
                dve.scalar_tensor_tensor(la[:, t, :], A[t][:], 0.0, las[:, t, :], ALU.min, ALU.subtract).then_inc(la_ready, 1)
            ada_unit_1(0, N_GLA + GA_AT[1], 1)
            for i, u in enumerate((1, 3)):
                wait_used(dve, 0, N_GLA + GW_AT[u])
                dve.wait_ge(decay_ready, 18 if i else 2)
                for g in range(2):
                    b, c = G[2 * i + g][:].rearrange("p (h s) -> p h s", h=2), slice(2 * g, 2 * g + 2)
                    if i == 0:
                        for dst, e in ((qf, epos), (qb, eneg)):
                            dve.scalar_tensor_tensor(dst[:, c, :], b, GLA_SCALE, e[:, c, :], ALU.mult, ALU.mult).then_inc(qkm_ready, 1)
                    else:
                        for dst, e in ((kf, eneg), (kb, epos), (ke, eend)):
                            dve.tensor_tensor(dst[:, c, :], b, e[:, c, :], ALU.mult).then_inc(qkm_ready, 1)
            for a in (2, 3):
                ada_unit_1(0, N_GLA + GA_AT[a], a)
            dve.wait_ge(att_zero, 1)
            for t in range(NT):
                dve.wait_ge(attp_ready, t + 1)
                for i, m in enumerate((lower, upper)):
                    if i:
                        dve.wait_ge(att_ready, 2 * t + 1)
                    dve.copy_predicated(att[:, :, t, :], m.unsqueeze(1).to_broadcast([P, H, P]),
                                        A[2 * t + i][:].rearrange("p (h q) -> p h q", h=H)).then_inc(att_ready, 1)
            for c, (b0, b1) in ((1, G[2:4]), (2, G[0:2])):
                dve.wait_ge(stp_ready, c + 1)
                if c == 1:
                    dve.wait_ge(st0_ready, 2)
                else:
                    dve.wait_ge(st_ready, H)
                for h in range(H):
                    e = (c + 1) * CHUNK - 1
                    dve.scalar_tensor_tensor(state[:, c, h, :], state[:, c - 1, h, :], epos[:, h, e:e + 1],
                                             (b0, b1)[h // 2][:, (h % 2) * S:(h % 2 + 1) * S], ALU.mult,
                                             ALU.add).then_inc(st_ready, 1)
            for a in (4, 5):
                ada_unit_1(0, N_GLA + GA_AT[a], a)
            dve.wait_ge(og_sq, 8)
            dve.tensor_scalar(ms[:], ss[:], 1.0 / S, EPS, ALU.mult, ALU.add).then_inc(ms_ready.sem, 1)
            inv_root(RE + 1, 8)
            for t in range(NT):
                for h in range(H):
                    dve.tensor_scalar(xs[:, t, h * S:(h + 1) * S], A[2 * t + h // 2][:, (h % 2) * S:(h % 2 + 1) * S],
                                      rs[:, 4 * t + h:4 * t + h + 1], None, ALU.mult).then_inc(og_ready, 1)
            for q in range(4):
                dve.wait_ge(ogp_ready, q + 1)
                for i in range(2):
                    c = 2 * q + i
                    dve.scalar_tensor_tensor(yT[:, c, :], G[q][:, i * S:(i + 1) * S], colb[:, B_GN + c:B_GN + c + 1],
                                             gateT[:, c, :], ALU.mult, ALU.mult).then_inc(yg_ready, 1)
            for a in (6, 7):
                ada_unit_1(0, N_GLA + GA_AT[a], a)
            deep_norm(0, N_GLA + GW_AT[14], N_GLA + GW_AT[15])
            stage_input(1)
            ada_unit_1(0, N_GLA + GA_AT[8], 8)
            square(1, 0, 0)
            with dve.Fori(0, 5) as i:
                ch.enter(i, 3 * (KC - 1))
                for k in range(3):
                    square(1, 3 * i + 1 + k, (k + 1) % 3)
                    ada_unit_1(3 * i, N_FF0 + 3 + 3 * k, AG + 3 * i + k)
            ch.leave(5)
            deep_norm(1, None, N_ATT - 1)
            coefficients(1)
            stage_input(2)

            def queries(qd):
                dve.wait_ge(bc_ready.sem, bc_ready.at(qd, 1))
                wait_used(dve, qd, N_ATT)
                for c in range(2):
                    dve.tensor_scalar(qk4[:, 0, c, :], G[0][:, c * S:(c + 1) * S], bcur[:, c:c + 1], HD_SCALE,
                                      ALU.add, ALU.mult).then_inc(qa_ready.sem, 1)

            def four_heads(qd, more=True):
                h0 = HE + H * qd
                dve.wait_ge(cur_ready.sem, cur_ready.at(qd, 2))
                for j in range(H):
                    head_max(h0, j, (A[1], A[2]), tcur[:, j, :], 1.0, True)
                    if j == 1:
                        wait_used(dve, qd, N_ATT + 2)
                        for t in range(NT):
                            dve.tensor_tensor(v4[:, t, :], G[2][:, t * GW:(t + 1) * GW], vcur[:], ALU.add).then_inc(v4_ready.sem, 1)
                    if j >= 1:
                        head_norm(h0, j - 1)
                head_norm(h0, H - 1)
                if more:
                    queries(qd + 1)
                dve.wait_ge(pv_ready.sem, h0 + H)
                dve.tensor_scalar(yT[:, bass.ds(2 * qd, 2), :], G[3][:].rearrange("p (c s) -> p c s", c=2), 1.0, None,
                                  ALU.mult).then_inc(oq_ready.sem, 1)

            queries(0)
            gate_rows(1)
            with dve.Fori(0, H - 1) as qd:
                ch.enter(qd, ATT_STEPS)
                four_heads(qd)
            ch.leave(H - 1)
            four_heads(H - 1, more=False)
            deep_norm(2, N_FF1 - 2, N_FF1 - 1)
            stage_input(3)
            square(3, 0, 0)
            with dve.Fori(0, 5) as i:
                for k in range(3):
                    square(3, 3 * i + 1 + k, (k + 1) % 3)
            deep_norm(3, None, N_FF1 + 2 * GROUPS - 1)
            dve.wait_ge(xn_ready.sem, xn_ready.at(3, 2))
            dve.wait_ge(lnrow_in, 64)
            for t in range(NT):
                ch.do(dve.tensor_tensor(xt[:, t, :], xs[:, t, :], ln_row[:, 0, :], ALU.mult))
            ch.sync()
            dve.tensor_tensor(xt[:], xt[:], ln_row[:, 1, :].unsqueeze(1).to_broadcast([P, NT, D]), ALU.add).then_inc(xu_ready.sem, 1)

        @block.tensor
        def _(pe):
            def unit_t(turns, n, act_t, b, stage=None):
                s = n % SLOTS
                wait_landed(pe, turns, n)
                for c in range(2):
                    for k in range(KC):
                        if c == 0 and stage is not None:
                            wait_input(stage, k)
                        mm = pe.matmul(b[:, c * S:(c + 1) * S], raw[:, s, k * 256 + c * P:k * 256 + (c + 1) * P],
                                       act_t[:, k, :], start=(k == 0), stop=(k == KC - 1))
                mm.then_inc(used[s], 1)

            def unit_n(turns, n, act_t, banks, half, width=512):
                s = n % SLOTS
                wait_landed(pe, turns, n)
                for t in range(NT):
                    for k in range(4):
                        mm = pe.matmul(banks[t][:, 0:width], act_t[:, 4 * half + k, t * P:(t + 1) * P],
                                       raw[:, s, k * 512:k * 512 + width],
                                       start=(half == 0 and k == 0), stop=(half == 1 and k == 3))
                mm.then_inc(used[s], 1)

            def scores(h0, j, b, q, k, again=False):
                if j >= 2 or again:
                    pe.wait_ge(nm_ready.sem, h0 + j - 1)
                pe.matmul(b[:, 0:P], q[:, 0:P], k[:, 0:P], start=True, stop=True)
                pe.matmul(b[:, P:384], q[:, P:S], k, start=True, stop=True).then_inc(score_ready.sem, 1)

            def turn(h0, j, banks, again=False):
                b = banks[j % 2]
                pe.wait_ge(pn_ready.sem, h0 + j + 1)
                if j >= 2 or again:
                    pe.wait_ge(pt_ready.sem, h0 + j - 1)
                for i in range(3):
                    mm = pe.transpose(b[:, i * P:(i + 1) * P], probs[:, j % 2, i * P:(i + 1) * P], ident)
                mm.then_inc(ptp_ready.sem, 1)

            def values(h0, j, b, v0, v1):
                h = j % H
                o = b[HD * (h % 2):HD * (h % 2) + HD, :]
                c = (h // 2) * S
                pe.wait_ge(pt_ready.sem, h0 + j + 1)
                pe.matmul(o[:, c:c + S], v0, probsT[:, j % 2, 0:S], start=True, stop=False)
                pe.matmul(o[:, c + P:c + S], v1, probsT[:, j % 2, S:384], start=False, stop=True).then_inc(pv_ready.sem, 1)

            pe.wait_ge(rel_in, 32)
            pe.wait_ge(relb_in, 16)
            pe.matmul(G[0][0:H, 0:384], relb[:], oneh[:], start=True, stop=True).then_inc(rr_psum, 1)
            pe.wait_ge(rr_ready, 1)
            with pe.Fori(0, DEPTH) as l:
                pe.wait_ge(xs_ready.sem, xs_ready.at(l, 2))
                for q in range(4):
                    for i in range(2):
                        for t in range(NT):
                            mm = pe.transpose(G[q][:, i * S + t * P:i * S + (t + 1) * P],
                                              xs[:, t, (2 * q + i) * P:(2 * q + i + 1) * P], ident)
                    mm.then_inc(htp_ready.sem, 1)
                pe.wait_ge(ht_act.sem, ht_act.at(l, 4))
                pe.wait_ge(ht_dve.sem, ht_dve.at(l, 4))
                unit_n(T1 * l, U_MLA0, hT, A[0:2], 0, MLA_IN)
                unit_n(T1 * l, U_MLA1, hT, A[0:2], 1, MLA_IN)
                unit_t(T1 * l, U_CA, hT, G[0])
                unit_t(T1 * l, U_CG, hT, G[1])
                unit_t(T1 * l, U_G0, hT, G[2])
                unit_t(T1 * l, U_G1, hT, G[3])
                pe.wait_ge(cn_ready.sem, cn_ready.at(l, 4))
                for t in range(NT):
                    c = slice(t * P, (t + 1) * P)
                    pe.transpose(A[2][:, c], cn[:, t, 0:P], ident)
                    pe.transpose(A[2][:, S + t * P:S + (t + 1) * P], cn[:, t, QR:QR + KVR], ident)
                    mm = pe.transpose(A[3][0:QR - P, c], cn[:, t, P:QR], ident)
                mm.then_inc(cnp_ready.sem, 1)
                pe.wait_ge(xg_ready.sem, xg_ready.at(l, 1))
                unit_t(T1 * l, U_G2, hT, G[0])
                unit_t(T1 * l, U_G3, hT, G[1])
                pe.wait_ge(silu_ready.sem, silu_ready.at(l, 2))
                unit_t(T1 * l, U_BQ, hT, G[2])
                unit_t(T1 * l, U_BK, hT, G[3])
                pe.wait_ge(ct_ready.sem, ct_ready.at(l, 3))
                for t in range(NT):
                    c = slice(t * P, (t + 1) * P)
                    pe.matmul(A[t][:, 0:H * QD], cT[:, 0, c], sm[:, M_UQ:M_UQ + H * QD], start=True, stop=False)
                    mm = pe.matmul(A[t][:, 0:H * QD], cT[0:QR - P, 1, c], sm[0:QR - P, M_UQ + 384:M_UQ + 384 + H * QD],
                                   start=False, stop=True)
                mm.then_inc(up_ready.sem, 1)
                for t in range(NT):
                    mm = pe.matmul(A[2 + t][:], cT[:, 2, t * P:(t + 1) * P], sm[:, M_UKV:M_UKV + 512], start=True, stop=True)
                mm.then_inc(up_ready.sem, 1)
                pe.wait_ge(silu_ready.sem, silu_ready.at(l, 4))
                unit_n(T1 * l, U_V0, hT, G[0:2], 0)
                unit_n(T1 * l, U_V1, hT, G[0:2], 1)
                pe.wait_ge(qk_ready.sem, qk_ready.at(l, 2))
                pe.wait_ge(upc_ready.sem, upc_ready.at(l, 2))
                for h in range(H):
                    r = slice(HD * (h % 2), HD * (h % 2) + HD)
                    mm = pe.matmul(G[2 + h % 2][:, (h // 2) * S:(h // 2 + 1) * S], qkB[r, 1, h // 2, 0:P],
                                   qkB[r, 0, h // 2, :], start=True, stop=True)
                mm.then_inc(z_ready.sem, 1)
                for h in range(H):
                    r = slice(HD * (h % 2), HD * (h % 2) + HD)
                    mm = pe.matmul(A[h % 2][:, (h // 2) * P:(h // 2 + 1) * P], qkB[r, 1, h // 2, P:S],
                                   qkB[r, 0, h // 2, P:S], start=True, stop=True)
                mm.then_inc(z_ready.sem, 1)
                pe.wait_ge(v_ready.sem, v_ready.at(l, 2))
                unit_t(T1 * l, U_CQ, hT, G[0])
                unit_t(T1 * l, U_CK, hT, G[1])
                pe.wait_ge(rope_ready.sem, rope_ready.at(l, 4))
                pe.wait_ge(upc_ready.sem, upc_ready.at(l, 6))
                for i, (src, h0, b) in enumerate(((qn, 0, A[2]), (qn, 2, A[3]), (kn, 0, A[1]), (kn, 2, A[2]))):
                    if i == 2:
                        pe.wait_ge(nl_ready.sem, nl_ready.at(l, 3))
                    if i == 3:
                        pe.wait_ge(qkT_ready.sem, qkT_ready.at(l, 1))
                    for h in range(2):
                        for t in range(NT):
                            mm = pe.transpose(b[0:QD, h * S + t * P:h * S + (t + 1) * P], src[:, t, h0 + h, :], ident)
                    mm.then_inc(qkp_ready.sem, 1)
                for i in range(3):
                    pe.wait_ge(nl_ready.sem, nl_ready.at(l, i + 1))
                for g in range(2):
                    pe.matmul(G[2 + g][:], uneg, nl[:, g * 512:(g + 1) * 512], start=True, stop=False)
                    later = G[2 + g][:].rearrange("p (h q) -> p h q", h=2)[:, :, P:S]
                    pe.matmul(later, oneg, nl[:, 1024 + g * 2 * P:1024 + (g + 1) * 2 * P], start=False,
                              stop=True).then_inc(sfx_ready.sem, 1)
                pe.matmul(A[0][:], uneg, nl[:, 1024:1536], start=True, stop=True).then_inc(sfx_ready.sem, 1)
                pe.wait_ge(qkT_ready.sem, qkT_ready.at(l, 4))
                pe.wait_ge(qk_ready.sem, qk_ready.at(l, 4))

                def head_scores(j):
                    h = j % H
                    if j < H:
                        scores(8 * l, j, A[1 + j % 2], qT[0:QD, h, :], kT[0:QD, h, :])
                    else:
                        r = slice(HD * (h % 2), HD * (h % 2) + HD)
                        scores(8 * l, j, A[1 + j % 2], qkC[r, 0, h // 2, :], qkC[r, 1, h // 2, :])

                def head_values(j):
                    h = j % H
                    if j < H:
                        values(8 * l, j, G[0], va[:, 0, h, :], va[:, 1, h, :])
                    else:
                        c = slice(GW + h * HD, GW + (h + 1) * HD)
                        values(8 * l, j, G[3], vBC[:, 0, c], vBC[:, 1, c])

                head_scores(0)
                head_scores(1)
                pe.wait_ge(lbs_ready.sem, lbs_ready.at(l, 3))
                for j in range(2 * H):
                    turn(8 * l, j, (A[3], A[0]))
                    if j + 2 < 2 * H:
                        head_scores(j + 2)
                    if j >= 1:
                        head_values(j - 1)
                    if j == 0:
                        pe.wait_ge(conv_ready.sem, conv_ready.at(l, 2))
                        for t in range(NT):
                            for c in range(2):
                                mm = pe.transpose(G[2][:, t * GW + c * P:t * GW + (c + 1) * P],
                                                  cacc[:, c, t * P:(t + 1) * P], ident)
                        mm.then_inc(cvp_ready.sem, 1)
                    if j == 2:
                        pe.wait_ge(at_ready.sem, at_ready.at(l, 2))
                        for h in range(H):
                            z = ZPOS[h]
                            o = G[1][HD * (h % 2):HD * (h % 2) + HD, :]
                            c = (h // 2) * S
                            pe.matmul(o[:, c:c + S], vBC[:, 0, h * HD:(h + 1) * HD], spl[:, z * S:(z + 1) * S],
                                      start=True, stop=False)
                            mm = pe.matmul(o[:, c + P:c + S], vBC[:, 1, h * HD:(h + 1) * HD],
                                           spl[:, 1024 + z * P:1024 + (z + 1) * P], start=False, stop=True)
                        mm.then_inc(osb_ready.sem, 1)
                    if j == 5:
                        pe.wait_ge(cnat_ready.sem, cnat_ready.at(l, 2))
                        for c in range(2):
                            for t in range(NT):
                                mm = pe.transpose(G[2][:, c * S + t * P:c * S + (t + 1) * P],
                                                  cnat[:, t, c * P:(c + 1) * P], ident)
                        mm.then_inc(cvp_ready.sem, 1)
                pe.wait_ge(y_ready.sem, y_ready.at(l, 2))
                unit_n(T1 * l, U_O0, yT, G[0:2], 0)
                head_values(2 * H - 1)
                pe.wait_ge(z_conv.sem, z_conv.at(l, 2))
                for e in range(2):
                    for c in range(2):
                        mm = pe.matmul(G[2][:, e * S:(e + 1) * S], sm[:, M_PW + c * GW + e * P:M_PW + c * GW + (e + 1) * P],
                                       zT[:, c, :], start=(c == 0), stop=(c == 1))
                mm.then_inc(cvp_ready.sem, 1)
                pe.wait_ge(y_ready.sem, y_ready.at(l, 5))
                unit_n(T1 * l, U_O1, yT, G[2:4], 0)
                unit_n(T1 * l, U_O2, yT, G[0:2], 1)
                unit_n(T1 * l, U_O3, yT, G[2:4], 1)

            def modulation(lay):
                wait_used(pe, 0, (N_GLA - 1, N_ATT - 2)[lay])
                for m, part in enumerate((0, 1, 3, 4)):
                    for j in range(KC):
                        c = part * D + j * P
                        mm = pe.matmul(A[0][:, m * KC + j:m * KC + j + 1], ada[:, c:c + P], ones[:, 0:1], start=True, stop=True)
                mm.then_inc(modc_psum.sem, 1)
                for b, c in ((A[1], 2 * D), (A[2], 2 * D + 512), (A[3], 5 * D), (A[0], 5 * D + 512)):
                    if b is A[0]:
                        pe.wait_ge(modc_used.sem, modc_used.at(lay, 1))
                    mm = pe.matmul(b[:], ones, ada[:, c:c + 512], start=True, stop=True)
                    if b is A[3] or b is A[0]:
                        mm.then_inc(modr_psum.sem, 1)

            def stage_input(s, src):
                for t in range(NT):
                    if s > 0:
                        pe.wait_ge(xn_ready.sem, xn_ready.at(s - 1, t + 1))
                    for q in range(4):
                        for i in range(2):
                            mm = pe.transpose(G[q][:, i * S + t * P:i * S + (t + 1) * P],
                                              src[:, t, (2 * q + i) * P:(2 * q + i + 1) * P], ident)
                        if t == NT - 1:
                            mm.then_inc(tp_ready.sem, 1)

            def wait_input(s, k):
                if k < 4:
                    pe.wait_ge(u_act.sem, u_act.at(s, k + 1))
                else:
                    pe.wait_ge(u_dve.sem, u_dve.at(s, k - 3))

            def second_product(s, turns, n, g, k, stop=False):
                wait_landed(pe, turns, n)
                pe.wait_ge(hid_ready.sem, hid_ready.at(s // 2, g + 1))
                for h in range(2):
                    for t in range(NT):
                        for c in range(2):
                            mm = pe.matmul(G[2 * h + t][:], hid[:, k, c, t * P:(t + 1) * P],
                                           raw[:, n % SLOTS, c * D + h * 512:c * D + (h + 1) * 512],
                                           start=False, stop=stop and c == 1)
                    if stop and h == 0:
                        mm.then_inc(y_half.sem, 1)
                mm.then_inc(used[n % SLOTS], 1)

            def net(s, n0, per):
                unit_t(0, n0, hT, A[0], s)
                for b in G:
                    pe.matmul(b[:], zeros[:, 0:P], zeros[:], start=True, stop=False)
                with pe.Fori(0, 5) as i:
                    for k in range(3):
                        n = n0 + 1 + (per // 3) * k
                        unit_t((per // SLOTS) * i, n, hT, A[(k + 1) % 3])
                        second_product(s, (per // SLOTS) * i, n + 1, 3 * i + k, k)
                second_product(s, 0, n0 + 1 + 5 * per, GROUPS - 1, 0, True)

            modulation(0)
            pe.wait_ge(x_new.sem, 2 * DEPTH + 2)
            stage_input(0, xt)
            pe.wait_ge(gla_in, 32)
            pe.wait_ge(u_dve.sem, 4)
            for k in range(KC):
                wait_input(0, k)
                mm = pe.matmul(G[3][0:16, 0:S], wlow[:, k, :], hT[:, k, :], start=(k == 0), stop=(k == KC - 1))
            mm.then_inc(lowp_ready, 1)
            for w in range(2):
                unit_t(0, N_GLA + GW_AT[w], hT, G[w])
            pe.wait_ge(low_ready, 1)
            pe.wait_ge(gate_used.sem, 2)
            for t in range(NT):
                mm = pe.matmul(A[t][:], low[0:17, t * P:(t + 1) * P], wgk[0:17, :], start=True, stop=True)
            mm.then_inc(lgp_ready, 1)
            for w in range(2, 4):
                unit_t(0, N_GLA + GW_AT[w], hT, G[w])
            pe.wait_ge(la_ready, 2)
            for h in range(H):
                for t in range(NT):
                    mm = pe.matmul(A[h // 2][:, (h % 2) * S + t * P:(h % 2) * S + (t + 1) * P], la[:, t, h * P:(h + 1) * P],
                                   cummat, start=True, stop=True)
            mm.then_inc(cump_ready, 1)
            for half in range(2):
                unit_n(0, N_GLA + GW_AT[4 + half], hT, A[2:4], half)
            pe.wait_ge(cum_ready, 2)
            for half in range(2):
                unit_n(0, N_GLA + GW_AT[6 + half], hT, A[0:2], half)
            for g in range(2):
                pe.wait_ge(qkm_ready, 2 * g + 2)
                unit_t(0, N_GLA + GW_AT[8 + g], hT, G[g])
            pe.wait_ge(qkm_ready, 10)
            pe.wait_ge(vg_ready, 4)
            for t in range(NT):
                c = slice(t * P, (t + 1) * P)
                for i, (k, q) in enumerate(((kf, qf), (kb, qb))):
                    for h in range(H):
                        mm = pe.matmul(A[2 * t + i][:, h * P:(h + 1) * P], k[:, h, c], q[:, h, c], start=True, stop=True)
                mm.then_inc(attp_ready, 1)
            for t in range(NT):
                for h in range(H):
                    mm = pe.transpose(G[2 + t][:, h * P:(h + 1) * P], ke[:, h, t * P:(t + 1) * P], ident)
            mm.then_inc(kep_ready, 1)
            pe.wait_ge(gate_ready, 2)
            pe.wait_ge(ken_ready, 2)
            for c, b in ((0, G[0:2]), (1, G[2:4]), (2, G[0:2])):
                if c == 2:
                    pe.wait_ge(st0_ready, 2)
                r = slice(CHUNK * (c % 2), CHUNK * (c % 2) + CHUNK)
                for h in range(H):
                    mm = pe.matmul(b[h // 2][:, (h % 2) * S:(h % 2 + 1) * S], ken[r, c // 2, h, :],
                                   vg[r, c // 2, h * S:(h + 1) * S], start=True, stop=True)
                mm.then_inc(stp_ready, 1)
            pe.wait_ge(att_ready, 4)
            pe.wait_ge(st_ready, 8)
            for t in range(NT):
                for h in range(H):
                    o = A[2 * t + h // 2][:, (h % 2) * S:(h % 2 + 1) * S]
                    if t > 0:
                        pe.matmul(o, att[:, h, t, :], vg[:, t, h * S:(h + 1) * S], start=True, stop=False)
                    for c in range(2 * t, 2 * t + 2):
                        r = slice(CHUNK * (c % 2), CHUNK * (c % 2) + CHUNK)
                        if t == 0:
                            mm = pe.matmul(o[r, :], att[:, h, t, r], vg[:, t, h * S:(h + 1) * S], start=True, stop=c == 0)
                        if c > 0:
                            mm = pe.matmul(o[r, :], qf[:, h, c * CHUNK:(c + 1) * CHUNK], state[:, c - 1, h, :],
                                           start=False, stop=True)
                mm.then_inc(og_psum, 1)
            for g in range(2, 4):
                unit_t(0, N_GLA + GW_AT[8 + g], hT, G[g])
            pe.wait_ge(og_ready, 8)
            for q in range(4):
                if q == 2:
                    pe.wait_ge(gate_ready, 4)
                for i in range(2):
                    for t in range(NT):
                        mm = pe.transpose(G[q][:, i * S + t * P:i * S + (t + 1) * P],
                                          xs[:, t, (2 * q + i) * P:(2 * q + i + 1) * P], ident)
                mm.then_inc(ogp_ready, 1)
            pe.wait_ge(yg_ready, 8)
            for w in range(4):
                unit_n(0, N_GLA + GW_AT[12 + w], yT, G[2 * (w % 2):2 * (w % 2) + 2], w // 2)
            stage_input(1, xs)
            pe.wait_ge(zeros_ready, 1)
            net(1, N_FF0, 9)
            modulation(1)
            stage_input(2, xs)

            def four_heads(qd, more=True):
                h0 = HE + H * qd

                def head_scores(j):
                    r = slice(HD * (j % 2), HD * (j % 2) + HD)
                    scores(h0, j, A[1 + j % 2], qk4[r, 0, j // 2, :], qk4[r, 1, j // 2, :], True)

                def head_values(j):
                    c = slice(j * HD, (j + 1) * HD)
                    values(h0, j, G[3], v4[:, 0, c], v4[:, 1, c])

                pe.wait_ge(qa_ready.sem, qa_ready.at(qd, 2))
                pe.wait_ge(ka_ready.sem, ka_ready.at(qd, 2))
                head_scores(0)
                head_scores(1)
                n = N_ATT + 2
                wait_landed(pe, qd, n)
                for t in range(NT):
                    for k in range(KC):
                        mm = pe.matmul(G[2][:, t * GW:(t + 1) * GW], hT[:, k, t * P:(t + 1) * P],
                                       raw[:, n % SLOTS, k * GW:(k + 1) * GW], start=(k == 0), stop=(k == KC - 1))
                mm.then_inc(used[n % SLOTS], 1)
                turn(h0, 0, (A[3], A[0]), True)
                head_scores(2)
                turn(h0, 1, (A[3], A[0]), True)
                head_scores(3)
                pe.wait_ge(v4_ready.sem, v4_ready.at(qd, 2))
                head_values(0)
                if more:
                    unit_t(qd + 1, N_ATT, hT, G[0])
                else:
                    pe.wait_ge(oq_ready.sem, 2)
                    unit_n(0, N_ATT + 12, yT, G[0:2], 0)
                turn(h0, 2, (A[3], A[0]), True)
                head_values(1)
                if more:
                    unit_t(qd + 1, N_ATT + 1, hT, G[1])
                turn(h0, 3, (A[3], A[0]), True)
                head_values(2)
                head_values(3)

            wait_input(2, 1)
            unit_t(0, N_ATT, hT, G[0], 2)
            unit_t(0, N_ATT + 1, hT, G[1])
            pe.wait_ge(gate_used.sem, 4)
            with pe.Fori(0, H - 1) as qd:
                four_heads(qd)
            four_heads(H - 1, more=False)
            pe.wait_ge(oq_ready.sem, H)
            for w in range(1, 4):
                unit_n(0, N_ATT + 12 + w, yT, G[2 * (w % 2):2 * (w % 2) + 2], w // 2)
            stage_input(3, xs)
            net(3, N_FF1, 6)


def constants():
    k = np.zeros((P, NCONST), np.float32)
    p, j = np.arange(P)[:, None], np.arange(S)[None, :]
    k[:, K_ID:K_ID + P] = np.eye(P)
    k[:, K_CAUSAL:K_CAUSAL + S] = np.where(P + p - j >= 0, 0.0, NEG)
    q = j[:, :P]
    k[:, K_KEEP:K_KEEP + P] = p < q
    k[:, K_UNEG:K_UNEG + P] = np.where(p > q, -1.0, 0.0)
    k[:, K_ONEG:K_ONEG + P] = -1.0
    k[:, K_ONE:K_ONE + P] = 1.0
    same = p // CHUNK == q // CHUNK
    k[:, K_CUM:K_CUM + P] = np.where(same & (p <= q), 1.0 / 16.0, 0.0)
    k[:, K_LOW:K_LOW + P] = same & (p <= q)
    k[:, K_UP:K_UP + P] = same & (p > q)
    freqs = np.float32(10000.0) ** (-np.arange(16, dtype=np.float32) / np.float32(16))
    ang = np.arange(S, dtype=np.float32)[:, None] * freqs[None, :]
    for t in range(NT):
        a = ang[t * P:(t + 1) * P].astype(np.float64)
        k[:, K_ROPE + 32 * t:K_ROPE + 32 * t + 16] = np.cos(a)
        k[:, K_ROPE + 32 * t + 16:K_ROPE + 32 * t + 32] = np.sin(a)
    return k


def bucket_lines():
    dist = np.arange(384) - (P - 1)
    n = np.maximum(dist, 0)
    exact = NB // 2
    large = exact + (np.log(np.maximum(n, exact).astype(np.float32) / np.float32(exact))
                     / np.float32(math.log(1024 / exact)) * np.float32(NB - exact)).astype(np.int32)
    b = np.where(n < exact, n, np.minimum(large, NB - 1))
    line = np.zeros((NB + 1, 384), np.float32)
    line[b, np.arange(384)] = (dist >= 0)
    line[NB] = np.where(dist >= 0, 0.0, NEG)
    return line


def t_unit(w, c0):
    return w[:, c0:c0 + 256].reshape(KC, P, 256).transpose(1, 0, 2).reshape(P, UNIT)


def n_unit(w, c0, half, width=512):
    u = np.zeros((P, 4, 512), w.dtype)
    u[:, :, :width] = w[half * 512:(half + 1) * 512, c0:c0 + width].reshape(4, P, width).transpose(1, 0, 2)
    return u.reshape(P, UNIT)


def ada_unit(w, a):
    return w[2 * (a % 4) * P:(2 * (a % 4) + 2) * P, (a // 4) * D:(a // 4 + 1) * D].reshape(2, P, D).transpose(1, 0, 2).reshape(P, UNIT)


def columns(v):
    n = -(-v.shape[0] // P)
    w = np.zeros((n * P,) + v.shape[1:], v.dtype)
    w[:v.shape[0]] = v
    return w.reshape(n, P).T


def lay_out(i):
    units = []
    sb0 = MLA_IN
    mo0 = sb0 + 3 * GW
    cv0 = mo0 + 3 * GW
    g0 = cv0 + 2 * GW
    cols, small = [], []
    for l in range(DEPTH):
        w, wo = i["w_in"][l], i["w_out"][l]
        v = np.concatenate([w[:, sb0 + 2 * GW:mo0], w[:, mo0 + 2 * GW:cv0]], 1)
        ws = [n_unit(w, 0, 0, MLA_IN), n_unit(w, 0, 1, MLA_IN), t_unit(w, cv0), t_unit(w, cv0 + GW)]
        ws += [t_unit(w, g0 + 256 * g) for g in range(4)]
        ws += [t_unit(w, sb0), t_unit(w, sb0 + GW), n_unit(v, 0, 0), n_unit(v, 0, 1)]
        ws += [t_unit(w, mo0), t_unit(w, mo0 + GW)]
        ws += [n_unit(wo, 512 * c, half) for half in range(2) for c in range(2)]
        layer = [None] * U1
        for n, u in zip(W_AT, ws):
            layer[n] = u
        for a, n in enumerate(A_AT):
            layer[n] = ada_unit(i["w_ada_2"][0], l * A1 + a)
        units += layer
        cols.append(np.concatenate([
            columns(i["pre_norm_g"][l]), columns(i["mla_q_norm_g"][l]), columns(i["mla_kv_norm_g"][l]),
            i["conv_dw_w"][l].reshape(TAPS, 2, P).transpose(2, 1, 0).reshape(P, 2 * TAPS),
            columns(i["conv_dw_b"][l]), columns(i["conv_ln_g"][l]), columns(i["conv_ln_b"][l]),
            columns(i["conv_pw_b"][l])], 1))
        uq = np.zeros((2 * P, H * QD), np.float32)
        uq[:QR] = i["mla_w_uq"][l]
        small.append(np.concatenate([
            uq.reshape(2, P, H * QD).transpose(1, 0, 2).reshape(P, 768), i["mla_w_ukv"][l],
            i["conv_pw_w"][l].reshape(2, P, GW).transpose(1, 0, 2).reshape(P, 512)], 1))
    ada1 = [t_unit(i["w_ada_2"][1], 256 * a) for a in range(6 * D // 256)]
    w, wo = i["gla_w_in_2"][0], i["gla_w_out_2"][0]
    ws = [t_unit(w, 256 * c) for c in range(4)]
    ws += [n_unit(w, 2 * GLA + 512 * c, half) for c in range(2) for half in range(2)]
    ws += [t_unit(w, 2 * GLA + D + 256 * c) for c in range(4)]
    ws += [n_unit(wo, 512 * c, half) for half in range(2) for c in range(2)]
    part = [None] * NG
    for n, u in zip(GW_AT + GA_AT, ws + ada1[:AG]):
        part[n] = u
    units += part
    for l in range(DEPTH):
        w1, w2 = i["ff_w1_2"][l], i["ff_w2_2"][l]
        f1 = [t_unit(w1, 256 * g) for g in range(GROUPS)]
        f2 = [w2[256 * g:256 * (g + 1)].reshape(2, P, D).transpose(1, 0, 2).reshape(P, UNIT) for g in range(GROUPS)]
        units.append(f1[0])
        for g in range(1, GROUPS):
            units += [f1[g], f2[g - 1]]
            if l == 0:
                units.append(ada1[AG + g - 1])
        units.append(f2[-1])
        if l == 0:
            w, wo = i["att_w_in_2"][0], i["att_w_out_2"][0]
            for qd in range(H):
                units += [t_unit(w, part * D + GW * qd) for part in range(3)]
            units += [n_unit(wo, 512 * c, half) for half in range(2) for c in range(2)]
    b_ada, b_in = i["b_ada_2"].reshape(DEPTH, 6, D), i["att_b_in_2"][0].reshape(3, D)
    ln_g, ln_b = i["ln_g_2"].reshape(2 * DEPTH, D), i["ln_b_2"].reshape(2 * DEPTH, D)
    qk = np.stack([b_in[0].reshape(H, 2, P), b_in[1].reshape(H, 2, P)], 1)
    colb = np.concatenate([columns(b_ada[:, [0, 1, 3, 4]].reshape(-1)), columns(ln_g[:3].reshape(-1)),
                           columns(ln_b[:3].reshape(-1)), columns(i["gla_g_norm_2"][0].reshape(-1)),
                           columns(qk.reshape(-1))], 1)
    low = i["gla_w_in_2"][0][:, 2 * GLA + 2 * D:]
    rb = i["att_rel_bias_2"][0]
    line = rb[:, np.clip(np.arange(384) - (P - 1), -P, P) + P]
    return {
        "x": i["x"], "units": np.stack(units), "cols": np.stack(cols), "small": np.stack(small),
        "post_g": i["post_norm_g"][:, None, :], "consts": constants(), "onehot": bucket_lines(),
        "rel_bias": i["rel_bias"], "ccol": columns(i["c_2"][0]),
        "colb": colb, "ada_rows": b_ada[:, [2, 5]].reshape(1, 4 * D), "ln_rows": np.stack([ln_g, ln_b], 1).reshape(4, 1, 2 * D),
        "low": low.reshape(KC, P, 16).transpose(1, 0, 2).reshape(P, KC * 16),
        "gk": np.concatenate([i["gla_w_gk2_2"][0], i["gla_b_gk_2"]], 0), "att_line": line,
        "v_row": b_in[2][None],
    }


def kernel(**inputs):
    import concourse.bacc as bacc
    from concourse.bass_utils import run_bass_kernel_spmd as run

    nc = bacc.Bacc("TRN2", target_bir_lowering=False, num_devices=1)
    arrays = {f"{n}_dram": np.ascontiguousarray(a) for n, a in lay_out({k: np.asarray(v) for k, v in inputs.items()}).items()}
    args = [nc.dram_tensor(n, a.shape, F32, kind="ExternalInput").ap() for n, a in arrays.items()]
    args.append(nc.dram_tensor("out_dram", (1, S, D), F32, kind="ExternalOutput").ap())
    build(nc, *args)
    return run(nc, [arrays], core_ids=[0]).results[0]["out_dram"]
```
